# Optimizing a Trainium2 kernel written in Bass

```python
import math
import jax, jax.numpy as jnp
from jax import lax
import numpy as np
import jax
import jax.numpy as jnp

D_MODEL = 2048
BATCH = 1
SEQ = 256
DEPTH = 2

GRID_W = 64
N_MIXERS = 2
HEAD_DIM = 128
A_HEADS = 16
A_KV_HEADS = 4
ROPE_THETA = 10000.0
A_Q_BLOCK = 128
A_QKV_WIDTH = (A_HEADS + 2 * A_KV_HEADS) * HEAD_DIM
B_GROUPS = ((128, 1), (512, 4), (2048, 16))
B_HEADS_PER_GROUP = 8
B_Q_BLOCK = 64
B_WIDTH = len(B_GROUPS) * B_HEADS_PER_GROUP * HEAD_DIM
B_QKV_WIDTH = 3 * B_WIDTH
REL_BUCKETS = 32
REL_MAX_DISTANCE = 1024
D_FF = 5632
CONV_WIDTH = 3
EPS = 1e-6
NEG_INF = -1e30
N_A_LAYERS = (DEPTH + 1) // 2
N_B_LAYERS = DEPTH // 2


def rms_norm(x, gain):
    xf = x.astype(jnp.float32)
    y = xf * lax.rsqrt(jnp.mean(xf * xf, axis=-1, keepdims=True) + EPS) * gain.astype(jnp.float32)
    return y.astype(x.dtype)

def axial_rope(x):
    seq = x.shape[1]
    rows = seq // GRID_W
    row_ids = jnp.repeat(jnp.arange(rows, dtype=jnp.float32), GRID_W)
    col_ids = jnp.tile(jnp.arange(GRID_W, dtype=jnp.float32), rows)
    half = HEAD_DIM // 2
    quarter = half // 2
    inv_freq = ROPE_THETA ** (-jnp.arange(quarter, dtype=jnp.float32) / quarter)

    def rot(xs, pos):
        ang = pos[:, None] * inv_freq[None, :]
        cos = jnp.cos(ang)[None, :, None, :]
        sin = jnp.sin(ang)[None, :, None, :]
        x1, x2 = xs[..., :quarter], xs[..., quarter:]
        return jnp.concatenate([x1 * cos - x2 * sin, x2 * cos + x1 * sin], axis=-1)

    return jnp.concatenate([rot(x[..., :half], row_ids), rot(x[..., half:], col_ids)], axis=-1)

def mixer_a(h, w_qkv, w_o, q_gain, k_gain):
    b, s, _ = h.shape
    qkv = h @ w_qkv
    nq = A_HEADS * HEAD_DIM
    nk = A_KV_HEADS * HEAD_DIM
    q = qkv[..., :nq].reshape(b, s, A_HEADS, HEAD_DIM)
    k = qkv[..., nq:nq + nk].reshape(b, s, A_KV_HEADS, HEAD_DIM)
    v = qkv[..., nq + nk:].reshape(b, s, A_KV_HEADS, HEAD_DIM)
    q = axial_rope(rms_norm(q.astype(jnp.float32), q_gain)).astype(h.dtype)
    k = axial_rope(rms_norm(k.astype(jnp.float32), k_gain)).astype(h.dtype)
    grp = A_HEADS // A_KV_HEADS
    nblk = s // A_Q_BLOCK
    qb = q.reshape(b, nblk, A_Q_BLOCK, A_KV_HEADS, grp, HEAD_DIM).transpose(1, 0, 2, 3, 4, 5)
    scale = HEAD_DIM ** -0.5

    def attend(q_blk):
        logits = jnp.einsum('bqkgd,bskd->bkgqs', q_blk, k).astype(jnp.float32) * scale
        p = jax.nn.softmax(logits, axis=-1).astype(v.dtype)
        return jnp.einsum('bkgqs,bskd->bqkgd', p, v)

    o = lax.map(attend, qb)
    o = o.transpose(1, 0, 2, 3, 4, 5).reshape(b, s, nq)
    return o @ w_o

def t5_bucket(rel):
    nb = REL_BUCKETS // 2
    max_exact = nb // 2
    base = jnp.where(rel > 0, nb, 0)
    n = jnp.abs(rel)
    nf = jnp.maximum(n, 1).astype(jnp.float32)
    large = max_exact + (jnp.log(nf / max_exact) / math.log(REL_MAX_DISTANCE / max_exact)
                         * (nb - max_exact)).astype(jnp.int32)
    large = jnp.minimum(large, nb - 1)
    return base + jnp.where(n < max_exact, n, large)

def dilated_group(q, k, v, rel_bias_g, window, dilation):
    b, s, h, d = q.shape
    half_span = window // (2 * dilation)
    L = s // dilation
    nblk = -(-L // B_Q_BLOCK)
    Lp = nblk * B_Q_BLOCK
    kv_len = B_Q_BLOCK + 2 * half_span
    qs = q.reshape(b, L, dilation, h, d)
    ks = k.reshape(b, L, dilation, h, d)
    vs = v.reshape(b, L, dilation, h, d)
    qs = jnp.pad(qs, ((0, 0), (0, Lp - L), (0, 0), (0, 0), (0, 0)))
    pad_kv = ((0, 0), (half_span, Lp - L + half_span), (0, 0), (0, 0), (0, 0))
    ks = jnp.pad(ks, pad_kv)
    vs = jnp.pad(vs, pad_kv)
    blk_start = jnp.arange(nblk) * B_Q_BLOCK
    key_idx = blk_start[:, None] + jnp.arange(kv_len)[None, :]
    kb = ks[:, key_idx]
    vb = vs[:, key_idx]
    qb = qs.reshape(b, nblk, B_Q_BLOCK, dilation, h, d)
    rel = jnp.arange(kv_len)[None, :] - half_span - jnp.arange(B_Q_BLOCK)[:, None]
    bias = rel_bias_g[t5_bucket(rel * dilation)].astype(jnp.float32).transpose(2, 0, 1)
    key_pos = key_idx - half_span
    valid = (jnp.abs(rel) <= half_span)[None] & ((key_pos >= 0) & (key_pos < L))[:, None, :]
    scale = d ** -0.5
    logits = jnp.einsum('bnqchd,bnkchd->bnchqk', qb, kb).astype(jnp.float32) * scale + bias[None, None, None]
    logits = jnp.where(valid[None, :, None, None], logits, NEG_INF)
    m = jnp.max(logits, axis=-1, keepdims=True)
    p = jnp.exp(logits - m)
    l = jnp.sum(p, axis=-1, keepdims=True)
    o = jnp.einsum('bnchqk,bnkchd->bnqchd', p.astype(v.dtype), vb).astype(jnp.float32)
    l_t = l[..., 0].transpose(0, 1, 4, 2, 3)
    o = o / l_t[..., None]
    log_z = (m[..., 0] + jnp.log(l[..., 0])).transpose(0, 1, 4, 2, 3)
    o = o.reshape(b, Lp, dilation, h, d)[:, :L].reshape(b, s, h, d)
    log_z = log_z.reshape(b, Lp, dilation, h)[:, :L].reshape(b, s, h)
    return o, log_z

def mixer_b(h, w_qkv, w_o, rel_bias):
    b, s, _ = h.shape
    n_g = len(B_GROUPS)
    hg = B_HEADS_PER_GROUP
    qkv = (h @ w_qkv).reshape(b, s, n_g, 3, hg, HEAD_DIM)
    outs, log_zs = [], []
    for g, (window, dil) in enumerate(B_GROUPS):
        o, lz = dilated_group(qkv[:, :, g, 0], qkv[:, :, g, 1], qkv[:, :, g, 2],
                              rel_bias[:, g * hg:(g + 1) * hg], window, dil)
        outs.append(o)
        log_zs.append(lz)
    wts = jax.nn.softmax(jnp.stack(log_zs, axis=0), axis=0)
    y = jnp.concatenate([wts[g][..., None] * outs[g] for g in range(n_g)], axis=2)
    y = y.reshape(b, s, B_WIDTH).astype(h.dtype)
    return y @ w_o

def conv_ffn(h, w_up, conv_w, conv_b, w_down):
    u = h @ w_up
    c = u.shape[-1]
    pad = CONV_WIDTH // 2
    u = lax.conv_general_dilated(u, conv_w[:, None, :].astype(u.dtype), window_strides=(1,),
                                 padding=((pad, pad),), dimension_numbers=('NWC', 'WIO', 'NWC'),
                                 feature_group_count=c) + conv_b
    gate, val = jnp.split(u, 2, axis=-1)
    return (jax.nn.silu(gate) * val) @ w_down

def first_inputs(seed: int = 0) -> dict:
    key = jax.random.key(seed)
    ks = jax.random.split(key, 16)
    f32 = jnp.float32
    nrm = lambda k, shape, sc: jax.random.normal(k, shape, f32) * sc
    return {
        "x": jax.random.normal(ks[0], (BATCH, SEQ, D_MODEL), f32),
        "a_w_qkv": nrm(ks[1], (N_A_LAYERS, D_MODEL, A_QKV_WIDTH), D_MODEL ** -0.5),
        "a_w_o": nrm(ks[2], (N_A_LAYERS, A_HEADS * HEAD_DIM, D_MODEL), (A_HEADS * HEAD_DIM) ** -0.5),
        "a_q_gain": 1.0 + nrm(ks[3], (N_A_LAYERS, HEAD_DIM), 0.02),
        "a_k_gain": 1.0 + nrm(ks[4], (N_A_LAYERS, HEAD_DIM), 0.02),
        "b_w_qkv": nrm(ks[5], (N_B_LAYERS, D_MODEL, B_QKV_WIDTH), D_MODEL ** -0.5),
        "b_w_o": nrm(ks[6], (N_B_LAYERS, B_WIDTH, D_MODEL), B_WIDTH ** -0.5),
        "rel_bias": nrm(ks[7], (REL_BUCKETS, len(B_GROUPS) * B_HEADS_PER_GROUP), 0.5),
        "mix_norm": 1.0 + nrm(ks[8], (DEPTH, D_MODEL), 0.02),
        "ffn_norm": 1.0 + nrm(ks[9], (DEPTH, D_MODEL), 0.02),
        "w_up": nrm(ks[10], (DEPTH, D_MODEL, 2 * D_FF), D_MODEL ** -0.5),
        "conv_w": nrm(ks[11], (DEPTH, CONV_WIDTH, 2 * D_FF), CONV_WIDTH ** -0.5),
        "conv_b": nrm(ks[12], (DEPTH, 2 * D_FF), 0.01),
        "w_down": nrm(ks[13], (DEPTH, D_FF, D_MODEL), D_FF ** -0.5),
        "final_norm": 1.0 + nrm(ks[14], (D_MODEL,), 0.02),
    }

def first_block(x, a_w_qkv, a_w_o, a_q_gain, a_k_gain, b_w_qkv, b_w_o, rel_bias,
              mix_norm, ffn_norm, w_up, conv_w, conv_b, w_down, final_norm):
    h = x
    for i in range(DEPTH):
        hn = rms_norm(h, mix_norm[i])
        j = i // N_MIXERS
        if i % N_MIXERS == 0:
            h = h + mixer_a(hn, a_w_qkv[j], a_w_o[j], a_q_gain[j], a_k_gain[j])
        else:
            h = h + mixer_b(hn, b_w_qkv[j], b_w_o[j], rel_bias)
        h = h + conv_ffn(rms_norm(h, ffn_norm[i]), w_up[i], conv_w[i], conv_b[i], w_down[i])
    return rms_norm(h, final_norm)


N_MIXERS_2 = 4
GROUP_WIDTH = D_MODEL // N_MIXERS_2
MIX_WIDTH = N_MIXERS_2 * GROUP_WIDTH
N_HEADS = GROUP_WIDTH // HEAD_DIM
Q_BLOCK = 128
RMS_EPS = 1e-6
NEG_INF_2 = -1e30

CMP_LEN = 32
CMP_STRIDE = 16
CMP_HIDDEN = HEAD_DIM
SEL_LEN = 64
SEL_TOPN = 16
WINDOW = 512
FORCED_BONUS = 1e6

MLA_Q_RANK = 384
MLA_KV_RANK = 128
MLA_NOPE = 128
MLA_ROPE = 64
MLA_V = 128

IN_SPLITS = (
    ("sb_q", GROUP_WIDTH), ("sb_k", GROUP_WIDTH), ("sb_v", GROUP_WIDTH), ("sb_gate", GROUP_WIDTH),
    ("nsa_q", GROUP_WIDTH), ("nsa_k_cmp", HEAD_DIM), ("nsa_v_cmp", HEAD_DIM),
    ("nsa_k_sel", HEAD_DIM), ("nsa_v_sel", HEAD_DIM), ("nsa_k_win", HEAD_DIM), ("nsa_v_win", HEAD_DIM),
    ("nsa_branch", 3 * N_HEADS), ("nsa_gate", GROUP_WIDTH),
    ("fox_q", GROUP_WIDTH), ("fox_k", GROUP_WIDTH), ("fox_v", GROUP_WIDTH), ("fox_f", N_HEADS),
    ("fox_gate", GROUP_WIDTH),
    ("mla_cq", MLA_Q_RANK), ("mla_ckv", MLA_KV_RANK), ("mla_k_rope", MLA_ROPE), ("mla_gate", GROUP_WIDTH),
)
IN_WIDTH = sum(width for _, width in IN_SPLITS)


def rms_norm_2(x, g):
    xf = x.astype(jnp.float32)
    y = xf * lax.rsqrt(jnp.mean(xf * xf, axis=-1, keepdims=True) + RMS_EPS)
    return (y * g.astype(jnp.float32)).astype(x.dtype)

def apply_rope(x, pos):
    half = x.shape[-1] // 2
    inv_freq = ROPE_THETA ** (-jnp.arange(half, dtype=jnp.float32) / half)
    ang = pos.astype(jnp.float32)[:, None] * inv_freq[None, :]
    cos = jnp.cos(ang)[:, None, :]
    sin = jnp.sin(ang)[:, None, :]
    xf = x.astype(jnp.float32)
    x1, x2 = xf[..., :half], xf[..., half:]
    return jnp.concatenate([x1 * cos - x2 * sin, x2 * cos + x1 * sin], axis=-1).astype(x.dtype)

def masked_softmax(z, mask):
    p = jax.nn.softmax(jnp.where(mask, z, NEG_INF_2), axis=-1)
    return jnp.where(mask, p, 0.0)

def sweep_query_blocks(block_fn, seq_len):
    out = lax.map(block_fn, jnp.arange(seq_len // Q_BLOCK))
    n_blocks, b, q, h, d = out.shape
    return jnp.moveaxis(out, 0, 1).reshape(b, n_blocks * q, h, d)

def split_columns(z):
    parts = {}
    offset = 0
    for name, width in IN_SPLITS:
        parts[name] = z[..., offset:offset + width]
        offset += width
    return parts

def stick_breaking_attention(q, k, v):
    B, S, H, d = q.shape
    scale = d ** -0.5
    kpos = jnp.arange(S)

    def block(i):
        s0 = i * Q_BLOCK
        qb = lax.dynamic_slice_in_dim(q, s0, Q_BLOCK, axis=1)
        qpos = s0 + jnp.arange(Q_BLOCK)
        z = jnp.einsum("bqhd,bshd->bhqs", qb, k).astype(jnp.float32) * scale
        earlier = kpos[None, :] < qpos[:, None]
        log_keep = jnp.where(earlier, jax.nn.log_sigmoid(-z), 0.0)
        log_after = lax.cumsum(log_keep, axis=3, reverse=True) - log_keep
        w = jnp.where(earlier, jnp.exp(jax.nn.log_sigmoid(z) + log_after), 0.0)
        return jnp.einsum("bhqs,bshd->bqhd", w.astype(v.dtype), v)

    return sweep_query_blocks(block, S)

def compress_blocks(tok, pos_emb, w1, w2):
    B, S, d = tok.shape
    n_cmp = (S - CMP_LEN) // CMP_STRIDE + 1
    gather = np.arange(n_cmp)[:, None] * CMP_STRIDE + np.arange(CMP_LEN)[None, :]
    blocks = tok[:, gather] + pos_emb
    hidden = jax.nn.silu(blocks.reshape(B, n_cmp, CMP_LEN * d) @ w1)
    return hidden @ w2

def native_sparse_attention(q, kc_tok, vc_tok, ks, vs, kw, vw, branch_gates,
                            pos_k, w1_k, w2_k, pos_v, w1_v, w2_v, pos):
    B, S, H, d = q.shape
    scale = d ** -0.5
    n_cmp = (S - CMP_LEN) // CMP_STRIDE + 1
    n_sel = S // SEL_LEN
    top_n = min(SEL_TOPN, n_sel)
    cmp_start = np.arange(n_cmp) * CMP_STRIDE
    cmp_end = jnp.asarray(cmp_start + CMP_LEN - 1, dtype=jnp.int32)
    sel_start = np.arange(n_sel) * SEL_LEN
    overlap = np.clip(np.minimum(cmp_start[:, None] + CMP_LEN, sel_start[None, :] + SEL_LEN)
                      - np.maximum(cmp_start[:, None], sel_start[None, :]), 0, None)
    cmp_to_sel = jnp.asarray(overlap / CMP_LEN, dtype=jnp.float32)

    q = apply_rope(q, pos)
    kc = compress_blocks(kc_tok, pos_k, w1_k, w2_k)
    kc = apply_rope(kc[:, :, None, :], cmp_end)[:, :, 0, :]
    vc = compress_blocks(vc_tok, pos_v, w1_v, w2_v)
    ks = apply_rope(ks[:, :, None, :], pos)[:, :, 0, :]
    kw = apply_rope(kw[:, :, None, :], pos)[:, :, 0, :]
    ks_blocks = ks.reshape(B, n_sel, SEL_LEN, d)
    vs_blocks = vs.reshape(B, n_sel, SEL_LEN, d)
    kw_pad = jnp.pad(kw, ((0, 0), (WINDOW, 0), (0, 0)))
    vw_pad = jnp.pad(vw, ((0, 0), (WINDOW, 0), (0, 0)))
    sel_ids = jnp.arange(n_sel)
    gather_blocks = jax.vmap(lambda blocks, ids: blocks[ids])

    def block(i):
        s0 = i * Q_BLOCK
        qb = lax.dynamic_slice_in_dim(q, s0, Q_BLOCK, axis=1)
        gb = lax.dynamic_slice_in_dim(branch_gates, s0, Q_BLOCK, axis=1)
        qpos = s0 + jnp.arange(Q_BLOCK)
        zc = jnp.einsum("bqhd,bnd->bhqn", qb, kc).astype(jnp.float32) * scale
        pc = masked_softmax(zc, cmp_end[None, :] <= qpos[:, None])
        o_cmp = jnp.einsum("bhqn,bnd->bqhd", pc.astype(vc.dtype), vc)
        imp = jnp.einsum("bhqn,ns->bqs", pc, cmp_to_sel)
        cur = qpos // SEL_LEN
        valid = sel_ids[None, :] <= cur[:, None]
        forced = ((sel_ids[None, :] == 0) | (sel_ids[None, :] == cur[:, None])
                  | (sel_ids[None, :] == cur[:, None] - 1))
        score = jnp.where(valid, jnp.where(forced, FORCED_BONUS, imp), NEG_INF_2)
        _, idx = lax.top_k(score, top_n)
        kg = gather_blocks(ks_blocks, idx)
        vg = gather_blocks(vs_blocks, idx).reshape(B, Q_BLOCK, top_n * SEL_LEN, d)
        tok = idx[..., None] * SEL_LEN + jnp.arange(SEL_LEN)
        sel_mask = (tok <= qpos[None, :, None, None]).reshape(B, 1, Q_BLOCK, top_n * SEL_LEN)
        zs = jnp.einsum("bqhd,bqnld->bhqnl", qb, kg).astype(jnp.float32)
        zs = zs.reshape(B, H, Q_BLOCK, top_n * SEL_LEN) * scale
        ps = masked_softmax(zs, sel_mask)
        o_slc = jnp.einsum("bhqm,bqmd->bqhd", ps.astype(vg.dtype), vg)
        kwb = lax.dynamic_slice_in_dim(kw_pad, s0, WINDOW + Q_BLOCK, axis=1)
        vwb = lax.dynamic_slice_in_dim(vw_pad, s0, WINDOW + Q_BLOCK, axis=1)
        kpos = s0 - WINDOW + jnp.arange(WINDOW + Q_BLOCK)
        win_mask = ((kpos[None, :] >= 0) & (kpos[None, :] <= qpos[:, None])
                    & (kpos[None, :] > qpos[:, None] - WINDOW))
        zw = jnp.einsum("bqhd,bkd->bhqk", qb, kwb).astype(jnp.float32) * scale
        pw = masked_softmax(zw, win_mask)
        o_win = jnp.einsum("bhqk,bkd->bqhd", pw.astype(vwb.dtype), vwb)
        return gb[..., 0:1] * o_cmp + gb[..., 1:2] * o_slc + gb[..., 2:3] * o_win

    return sweep_query_blocks(block, S)

def forgetting_attention(q, k, v, log_f):
    B, S, H, d = q.shape
    scale = d ** -0.5
    cum = jnp.cumsum(log_f, axis=1).transpose(0, 2, 1)
    kpos = jnp.arange(S)

    def block(i):
        s0 = i * Q_BLOCK
        qb = lax.dynamic_slice_in_dim(q, s0, Q_BLOCK, axis=1)
        cq = lax.dynamic_slice_in_dim(cum, s0, Q_BLOCK, axis=2)
        qpos = s0 + jnp.arange(Q_BLOCK)
        z = (jnp.einsum("bqhd,bshd->bhqs", qb, k).astype(jnp.float32) * scale
             + cq[..., None] - cum[:, :, None, :])
        p = masked_softmax(z, kpos[None, :] <= qpos[:, None])
        return jnp.einsum("bhqs,bshd->bqhd", p.astype(v.dtype), v)

    return sweep_query_blocks(block, S)

def latent_attention(c_q, c_kv, k_rope, q_norm_g, w_uq, kv_norm_g, w_ukv, pos):
    B, S, _ = c_q.shape
    q = (rms_norm_2(c_q, q_norm_g) @ w_uq).reshape(B, S, N_HEADS, MLA_NOPE + MLA_ROPE)
    q_nope = q[..., :MLA_NOPE]
    q_rot = apply_rope(q[..., MLA_NOPE:], pos)
    kv = (rms_norm_2(c_kv, kv_norm_g) @ w_ukv).reshape(B, S, N_HEADS, MLA_NOPE + MLA_V)
    k_nope, v = kv[..., :MLA_NOPE], kv[..., MLA_NOPE:]
    k_rot = apply_rope(k_rope[:, :, None, :], pos)[:, :, 0, :]
    scale = (MLA_NOPE + MLA_ROPE) ** -0.5
    kpos = jnp.arange(S)

    def block(i):
        s0 = i * Q_BLOCK
        qn = lax.dynamic_slice_in_dim(q_nope, s0, Q_BLOCK, axis=1)
        qr = lax.dynamic_slice_in_dim(q_rot, s0, Q_BLOCK, axis=1)
        qpos = s0 + jnp.arange(Q_BLOCK)
        z = (jnp.einsum("bqhd,bshd->bhqs", qn, k_nope)
             + jnp.einsum("bqhr,bsr->bhqs", qr, k_rot)).astype(jnp.float32) * scale
        p = masked_softmax(z, kpos[None, :] <= qpos[:, None])
        return jnp.einsum("bhqs,bshd->bqhd", p.astype(v.dtype), v)

    return sweep_query_blocks(block, S)

def hybrid_layer(x, pre_g, post_g, w_in, b_in, w_out, forget_bias,
                 pos_k, w1_k, w2_k, pos_v, w1_v, w2_v,
                 q_norm_g, w_uq, kv_norm_g, w_ukv):
    B, S, _ = x.shape
    pos = jnp.arange(S)
    h = rms_norm_2(x, pre_g)
    p = split_columns(h @ w_in + b_in)

    def heads(t):
        return t.reshape(B, S, N_HEADS, HEAD_DIM)

    o_sb = stick_breaking_attention(heads(p["sb_q"]), heads(p["sb_k"]), heads(p["sb_v"]))

    branch_gates = jax.nn.sigmoid(p["nsa_branch"].reshape(B, S, N_HEADS, 3))
    o_nsa = native_sparse_attention(heads(p["nsa_q"]), p["nsa_k_cmp"], p["nsa_v_cmp"],
                                    p["nsa_k_sel"], p["nsa_v_sel"], p["nsa_k_win"], p["nsa_v_win"],
                                    branch_gates, pos_k, w1_k, w2_k, pos_v, w1_v, w2_v, pos)

    log_f = jax.nn.log_sigmoid((p["fox_f"] + forget_bias).astype(jnp.float32))
    o_fox = forgetting_attention(heads(p["fox_q"]), heads(p["fox_k"]), heads(p["fox_v"]), log_f)

    o_mla = latent_attention(p["mla_cq"], p["mla_ckv"], p["mla_k_rope"],
                             q_norm_g, w_uq, kv_norm_g, w_ukv, pos)

    mix = jnp.concatenate([
        o_sb.reshape(B, S, GROUP_WIDTH) * jax.nn.silu(p["sb_gate"]),
        o_nsa.reshape(B, S, GROUP_WIDTH) * jax.nn.silu(p["nsa_gate"]),
        o_fox.reshape(B, S, GROUP_WIDTH) * jax.nn.silu(p["fox_gate"]),
        o_mla.reshape(B, S, GROUP_WIDTH) * jax.nn.silu(p["mla_gate"]),
    ], axis=-1)
    return x + rms_norm_2(mix @ w_out, post_g)

def second_inputs(seed: int = 0) -> dict:
    key = jax.random.key(seed)
    ks = jax.random.split(key, 17)
    f32 = jnp.float32

    def normal(k, shape, scale):
        return jax.random.normal(k, shape, f32) * scale

    def gain(k, shape):
        return 1.0 + 0.02 * jax.random.normal(k, shape, f32)

    flat = CMP_LEN * HEAD_DIM
    return {
        "x": normal(ks[0], (BATCH, SEQ, D_MODEL), 1.0),
        "pre_norm_g": gain(ks[1], (DEPTH, D_MODEL)),
        "post_norm_g": gain(ks[2], (DEPTH, D_MODEL)),
        "w_in": normal(ks[3], (DEPTH, D_MODEL, IN_WIDTH), D_MODEL ** -0.5),
        "b_in": normal(ks[4], (DEPTH, IN_WIDTH), 0.02),
        "w_out": normal(ks[5], (DEPTH, MIX_WIDTH, D_MODEL), MIX_WIDTH ** -0.5),
        "fox_forget_bias": jax.random.uniform(ks[6], (DEPTH, N_HEADS), f32, 1.0, 4.0),
        "nsa_cmp_pos_k": normal(ks[7], (DEPTH, CMP_LEN, HEAD_DIM), 0.02),
        "nsa_cmp_w1_k": normal(ks[8], (DEPTH, flat, CMP_HIDDEN), flat ** -0.5),
        "nsa_cmp_w2_k": normal(ks[9], (DEPTH, CMP_HIDDEN, HEAD_DIM), CMP_HIDDEN ** -0.5),
        "nsa_cmp_pos_v": normal(ks[10], (DEPTH, CMP_LEN, HEAD_DIM), 0.02),
        "nsa_cmp_w1_v": normal(ks[11], (DEPTH, flat, CMP_HIDDEN), flat ** -0.5),
        "nsa_cmp_w2_v": normal(ks[12], (DEPTH, CMP_HIDDEN, HEAD_DIM), CMP_HIDDEN ** -0.5),
        "mla_q_norm_g": gain(ks[13], (DEPTH, MLA_Q_RANK)),
        "mla_w_uq": normal(ks[14], (DEPTH, MLA_Q_RANK, N_HEADS * (MLA_NOPE + MLA_ROPE)), MLA_Q_RANK ** -0.5),
        "mla_kv_norm_g": gain(ks[15], (DEPTH, MLA_KV_RANK)),
        "mla_w_ukv": normal(ks[16], (DEPTH, MLA_KV_RANK, N_HEADS * (MLA_NOPE + MLA_V)), MLA_KV_RANK ** -0.5),
    }

def second_block(x, pre_norm_g, post_norm_g, w_in, b_in, w_out, fox_forget_bias,
              nsa_cmp_pos_k, nsa_cmp_w1_k, nsa_cmp_w2_k,
              nsa_cmp_pos_v, nsa_cmp_w1_v, nsa_cmp_w2_v,
              mla_q_norm_g, mla_w_uq, mla_kv_norm_g, mla_w_ukv):
    for l in range(DEPTH):
        x = hybrid_layer(x, pre_norm_g[l], post_norm_g[l], w_in[l], b_in[l], w_out[l],
                         fox_forget_bias[l],
                         nsa_cmp_pos_k[l], nsa_cmp_w1_k[l], nsa_cmp_w2_k[l],
                         nsa_cmp_pos_v[l], nsa_cmp_w1_v[l], nsa_cmp_w2_v[l],
                         mla_q_norm_g[l], mla_w_uq[l], mla_kv_norm_g[l], mla_w_ukv[l])
    return x


def setup_inputs(seed=0):
    out = dict(first_inputs(seed))
    for name, value in second_inputs(seed + 1).items():
        if name != "x":
            out[name + "_2"] = value
    return out


def reference(
    x, a_w_qkv, a_w_o, a_q_gain, a_k_gain, b_w_qkv, b_w_o, rel_bias, mix_norm, ffn_norm, w_up,
    conv_w, conv_b, w_down, final_norm, pre_norm_g_2, post_norm_g_2, w_in_2, b_in_2, w_out_2,
    fox_forget_bias_2, nsa_cmp_pos_k_2, nsa_cmp_w1_k_2, nsa_cmp_w2_k_2, nsa_cmp_pos_v_2,
    nsa_cmp_w1_v_2, nsa_cmp_w2_v_2, mla_q_norm_g_2, mla_w_uq_2, mla_kv_norm_g_2, mla_w_ukv_2,
):
    x = first_block(
        x, a_w_qkv, a_w_o, a_q_gain, a_k_gain, b_w_qkv, b_w_o, rel_bias, mix_norm, ffn_norm,
        w_up, conv_w, conv_b, w_down, final_norm,
    )
    return second_block(
        x, pre_norm_g_2, post_norm_g_2, w_in_2, b_in_2, w_out_2, fox_forget_bias_2,
        nsa_cmp_pos_k_2, nsa_cmp_w1_k_2, nsa_cmp_w2_k_2, nsa_cmp_pos_v_2, nsa_cmp_w1_v_2,
        nsa_cmp_w2_v_2, mla_q_norm_g_2, mla_w_uq_2, mla_kv_norm_g_2, mla_w_ukv_2,
    )


_drawn_inputs = setup_inputs


def setup_inputs(seed=0):
    import zlib

    import numpy as np

    out = dict(_drawn_inputs(seed))
    spreads = {}
    factors = {'a_q_gain': 8.0,
     'a_k_gain': 8.0,
     'mix_norm': 6.259,
     'conv_b': 3.063,
     'post_norm_g_2': 2.674,
     'nsa_cmp_pos_k_2': 55.004,
     'nsa_cmp_pos_v_2': 7.559,
     'mla_q_norm_g_2': 8.0,
     'mla_kv_norm_g_2': 8.0}
    for name, (base, spread) in spreads.items():
        noise = np.random.default_rng([zlib.crc32(name.encode()), seed]).standard_normal(out[name].shape)
        drawn = base * np.exp(spread * noise) if base else spread * noise
        out[name] = jnp.asarray(drawn.astype(out[name].dtype))
    for name, factor in factors.items():
        out[name] = (out[name] * factor).astype(out[name].dtype)
    return out
```

```python
from contextlib import ExitStack

import concourse.bass as bass
import numpy as np
from concourse import mybir

F32 = mybir.dt.float32
F32R = mybir.dt.float32r
ALU = mybir.AluOpType
ACT = mybir.ActivationFunctionType
AX_X = mybir.AxisListType.X

P = 128
TB = 2
S = TB * P
D = 2048
KT = D // P
FF = 5632
FFC = FF // P
EPS = 1e-6
NEG = -1e30
UNIT = 2048
RAW = 4
SPLIT = 2
AHEAD = 2
A_HEADS, A_KV = 16, 4
B_HEADS, B_GROUPS = 8, 3
H2 = 4
N_CMP = (S - 32) // 16 + 1
SKEW = P * (2 * S + 1)
FFN_PARTS = (16, 16, 12)
GAIN_MIX, GAIN_FFN, GAIN_PRE = 0, 2 * KT, 4 * KT
PARTS = (("sb", 2048, (512,) * 4), ("nsa", 1804, (452, 452, 450, 450)),
         ("fox", 2052, (412, 410, 410, 410, 410)), ("mla", 1088, (364, 364, 360)))
IN_WIDTH = sum(p[1] for p in PARTS)


def weight_units(w):
    units = []

    def rows(m, k0, nk, c0, nc_):
        return m[k0 * P:(k0 + nk) * P, c0:c0 + nc_].rearrange("(k p) n -> p k n", p=P)

    def by_column_group(m, k0, nk, widths):
        c0 = 0
        for wd in widths:
            for k in range(0, nk, 4):
                units.append(rows(m, k0 + k, 4, c0, wd))
            c0 += wd

    def ffn(layer):
        done = 0
        for part in FFN_PARTS:
            for j in range(part // 2):
                for half in range(2):
                    for k in (0, 8):
                        units.append(rows(w["w_up"][layer], k, 8, half * FF + (done + 2 * j) * P, 256))
            by_column_group(w["w_down"][layer], done, part, (512,) * 4)
            done += part

    by_column_group(w["a_w_qkv"][0], 0, KT, (512,) * 6)
    by_column_group(w["a_w_o"][0], 0, KT, (512,) * 4)
    ffn(0)
    for half in range(2):
        for pair in range(2):
            for g in range(B_GROUPS):
                for kind in range(3):
                    c0 = ((g * 3 + kind) * B_HEADS + half * 4 + pair * 2) * P
                    for k in (0, 8):
                        units.append(rows(w["b_w_qkv"][0], k, 8, c0, 256))
        for cg in range(4):
            for g in range(B_GROUPS):
                units.append(rows(w["b_w_o"][0], g * B_HEADS + half * 4, 4, cg * 512, 512))
    ffn(1)
    for layer in range(2):
        c0 = 0
        for _, width, cgs in PARTS:
            by_column_group(w["w_in_2"][layer][:, c0:c0 + width], 0, KT, cgs)
            c0 += width
        by_column_group(w["w_out_2"][layer], 0, KT, (512,) * 4)
    return units


class Core:
    pass


def make_core(nc, w, ctx):
    c = Core()
    c.nc, c.w = nc, w
    c.units = weight_units(w)
    c.u0 = 0
    c.stages = 0
    c.sems = ExitStack()

    def sb(name, shape, dt=F32):
        return ctx.enter_context(nc.sbuf_tensor(name, shape, dt))

    c.bank = [ctx.enter_context(nc.psum_tensor(f"bank{i}", [P, 512], F32)) for i in range(8)]
    c.raw = [sb(f"raw{i}", [P, UNIT]) for i in range(RAW)]
    c.high = [sb(f"high{i}", [P, UNIT], F32R) for i in range(SPLIT)]
    c.low = [sb(f"low{i}", [P, UNIT], F32R) for i in range(SPLIT)]
    c.x = sb("x", [P, TB, D])
    c.hh = sb("h_high", [P, KT, S], F32R)
    c.hl = sb("h_low", [P, KT, S], F32R)
    c.yh = sb("y_high", [P, KT, S], F32R)
    c.yl = sb("y_low", [P, KT, S], F32R)
    c.ident = sb("ident", [P, P])
    c.causal = sb("causal", [P, TB, S])
    c.gain = sb("gain", [P, 6 * KT])
    c.eps = sb("eps", [P, 1])
    c.conv_all = sb("conv", [P, 2 * 4 * 2 * FFC])
    c.conv = [c.conv_all[:, i * 8 * FFC:(i + 1) * 8 * FFC].rearrange("p (a k) -> p a k", a=4) for i in range(2)]
    c.small = [sb(f"small{i}", [P, 68]) for i in range(2)]
    c.arrived = [ctx.enter_context(nc.semaphore(f"w_arrived{i}")) for i in range(RAW)]
    c.w_high = ctx.enter_context(nc.semaphore("w_high"))
    c.w_low = ctx.enter_context(nc.semaphore("w_low"))
    c.preloaded = ctx.enter_context(nc.semaphore("preloaded"))
    c.n_preloads = 0
    c.skewed = ctx.enter_context(nc.semaphore("bias_skewed"))
    c.w_used = ctx.enter_context(nc.semaphore("w_used"))
    return c



def load_unit(c, sp, u, i=0, per=0, src=None):
    if src is None:
        if u >= len(c.units):
            return
        src = c.units[u]
    k, n = src.shape[1], src.shape[2]
    if u >= RAW:
        sp.wait_ge(c.w_low, u - RAW + 1 + i * per)
    dst = c.raw[u % RAW][:, 0:k * n].rearrange("p (k n) -> p k n", k=k)
    sp.dma_start(dst, src).then_inc(c.arrived[u % RAW], 16)


def split_high(c, act, u, i=0, per=0):
    if u >= len(c.units):
        return
    act.wait_ge(c.arrived[u % RAW], 16 * (u // RAW + 1) + i * (per // RAW * 16))
    if u >= SPLIT:
        act.wait_ge(c.w_used, u - SPLIT + 1 + i * per)
    n = c.units[u].shape[1] * c.units[u].shape[2]
    act.activation(c.high[u % SPLIT][:, 0:n], c.raw[u % RAW][:, 0:n], ACT.Copy).then_inc(c.w_high, 1)


def split_low(c, dve, u, i=0, per=0):
    if u >= len(c.units):
        return
    dve.wait_ge(c.w_high, u + 1 + i * per)
    n = c.units[u].shape[1] * c.units[u].shape[2]
    dve.tensor_tensor(c.low[u % SPLIT][:, 0:n], c.raw[u % RAW][:, 0:n],
                      c.high[u % SPLIT][:, 0:n].bitcast(F32), ALU.subtract).then_inc(c.w_low, 1)


def split_view(c, u):
    k, n = c.units[u].shape[1], c.units[u].shape[2]
    return [t[u % SPLIT][:, 0:k * n].rearrange("p (k n) -> p k n", k=k) for t in (c.high, c.low)]


def load_steps(c, sp, n):
    for j in range(n):
        load_unit(c, sp, c.u0 + j + RAW)


def three(pe, out, lh, ll, rh, rl, start, stop, skip=False):
    pe.matmul(out, lh, rh, start=start, stop=False, skip_group_check=skip)
    pe.matmul(out, lh, rl, start=False, stop=False, skip_group_check=skip)
    return pe.matmul(out, ll, rh, start=False, stop=stop, skip_group_check=skip)


class Chain:

    def __init__(self, eng, sem):
        self.eng, self.sem, self.n = eng, sem, 0

    def link(self, ins):
        self.n += 1
        ins.then_inc(self.sem, 1)
        self.eng.wait_ge(self.sem, self.n)


def stage(c):
    st = ExitStack()
    c.stages += 1
    tag = f"st{c.stages}_"

    def sb(name, shape, dt=F32):
        return st.enter_context(c.nc.sbuf_tensor(tag + name, shape, dt))

    before, c.sems = c.sems, ExitStack()
    sems = []

    def end():
        for s in sems:
            c.nc.gpsimd.sem_clear(s)
        before.close()

    def sem(name):
        sems.append(c.sems.enter_context(c.nc.semaphore(tag + name)))
        return sems[-1]

    st.callback(end)
    return st, sb, sem


def preload(c, sp, pairs):
    if pairs and c.n_preloads:
        sp.wait_ge(c.preloaded, 16 * c.n_preloads)
    for dst, src in pairs:
        sp.dma_start(dst, src).then_inc(c.preloaded, 16)
        c.n_preloads += 1


def await_preloads(c, eng):
    eng.wait_ge(c.preloaded, 16 * c.n_preloads)



def setup_stage(c, consts):
    st, sb, sem = stage(c)
    with st:
        gain_rows = sb("gain_rows", [6 * KT, P])
        conv_rows = sb("conv_rows", [2 * FFC, 2, 4, P])
        small_rows = sb("small_rows", [68, 2, P])
        x_loaded, g_loaded, s_loaded, c_loaded, turned = (sem(n) for n in (
            "x_loaded", "gains_loaded", "small_loaded", "conv_loaded", "turned"))
        block = st.enter_context(c.nc.Block())

        @block.sync
        def _(sp):
            sp.dma_start(c.ident[:, :], consts["ident"]).then_inc(g_loaded, 16)
            for name, at in (("mix_norm", GAIN_MIX), ("ffn_norm", GAIN_FFN), ("pre_norm_g_2", GAIN_PRE)):
                sp.dma_start(gain_rows[at:at + 2 * KT, :],
                             c.w[name].rearrange("l (k p) -> (l k) p", p=P)).then_inc(g_loaded, 16)
            sp.dma_start(c.x[:, :, :], c.w["x"][0].rearrange("(t p) d -> p t d", p=P)).then_inc(x_loaded, 16)
            for u in range(2):
                load_unit(c, sp, u)
            for i in range(2):
                sp.dma_start(small_rows[0:32, i, :], c.w["nsa_cmp_pos_k_2"][i]).then_inc(s_loaded, 16)
                sp.dma_start(small_rows[32:64, i, :], c.w["nsa_cmp_pos_v_2"][i]).then_inc(s_loaded, 16)
                sp.dma_start(small_rows[64:67, i, :], c.w["mla_q_norm_g_2"][i].rearrange("(k p) -> k p", p=P)).then_inc(s_loaded, 16)
                sp.dma_start(small_rows[67:68, i, :], c.w["mla_kv_norm_g_2"][i:i + 1, :]).then_inc(s_loaded, 16)
            for i in range(2):
                for tap in range(3):
                    sp.dma_start(conv_rows[:, i, tap, :],
                                 c.w["conv_w"][i, tap].rearrange("(k p) -> k p", p=P)).then_inc(c_loaded, 16)
                sp.dma_start(conv_rows[:, i, 3, :], c.w["conv_b"][i].rearrange("(k p) -> k p", p=P)).then_inc(c_loaded, 16)
            sp.dma_start(c.causal[:, :, :], consts["causal"]).then_inc(x_loaded, 16)
            for u in range(2, RAW):
                load_unit(c, sp, u)
            sp.wait_ge(x_loaded, 32)

        @block.scalar
        def _(act):
            split_high(c, act, 0)

        @block.vector
        def _(dve):
            dve.memset(c.eps[:, :], EPS)
            split_low(c, dve, 0)
            dve.wait_ge(turned, 1)
            dve.tensor_copy(c.gain[:, :], c.bank[0][:, 0:6 * KT])
            for i in range(2):
                dve.wait_ge(turned, 2 + i)
                dve.tensor_copy(c.small[i][:, :], c.bank[1 + i][:, 0:68])
            for i in range(2):
                dve.wait_ge(turned, 4 + i)
                dve.tensor_copy(c.conv[i][:, :, :], c.bank[3 + i][:, 0:8 * FFC].rearrange("p (a k) -> p a k", a=4))

        @block.tensor
        def _(pe):
            pe.wait_ge(g_loaded, 64)
            pe.transpose(c.bank[0][:, 0:6 * KT], gain_rows[:, :], c.ident[0:6 * KT, 0:6 * KT]).then_inc(turned, 1)
            pe.wait_ge(s_loaded, 128)
            for i in range(2):
                pe.transpose(c.bank[1 + i][:, 0:68], small_rows[:, i, :], c.ident[0:68, 0:68]).then_inc(turned, 1)
            pe.wait_ge(c_loaded, 128)
            for i in range(2):
                for a in range(4):
                    ins = pe.transpose(c.bank[3 + i][:, a * 2 * FFC:(a + 1) * 2 * FFC], conv_rows[:, i, a, :],
                                       c.ident[0:2 * FFC, 0:2 * FFC])
                ins.then_inc(turned, 1)



def norm_stage(c, gain_col, ahead=()):
    st, sb, sem = stage(c)
    half = D // 2
    with st:
        xn = sb("xn", [P, TB, D])
        stat = sb("stat", [P, 4, TB])
        squared, summed, inverted, rooted = sem("squared"), sem("summed"), sem("inverted"), sem("rooted")
        scaled = [sem(f"scaled{t}") for t in range(TB)]
        turned, high = sem("turned"), sem("high")
        block = st.enter_context(c.nc.Block())

        @block.sync
        def _(sp):
            preload(c, sp, ahead)

        @block.scalar
        def _(act):
            act.activation(xn[:, 0, :], c.x[:, 0, :], ACT.Square, accum_out=stat[:, 0, 0:1]).then_inc(squared, 1)
            act.wait_ge(inverted, 1)
            act.activation(stat[:, 3, :], stat[:, 2, :], ACT.Sqrt).then_inc(rooted, 1)
            act.wait_ge(rooted, 1)
            for h in range(2):
                cols = slice(h * half, (h + 1) * half)
                act.activation(xn[:, 1, cols], c.x[:, 1, cols], ACT.Copy, scale=stat[:, 3, 1:2]).then_inc(scaled[1], 1)
            for b in range(8):
                act.wait_ge(turned, b + 1)
                for k in range(2):
                    ins = act.activation(c.hh[:, 2 * b + k, :], c.bank[b][:, k * S:(k + 1) * S], ACT.Copy,
                                         scale=c.gain[:, gain_col + 2 * b + k:gain_col + 2 * b + k + 1])
                ins.then_inc(high, 1)

        @block.vector
        def _(dve):
            chain = Chain(dve, summed)
            chain.link(dve.tensor_tensor_reduce(xn[:, 1, :], c.x[:, 1, :], c.x[:, 1, :], 1.0, 0.0, ALU.mult,
                                                ALU.add, stat[:, 0, 1:2]))
            dve.wait_ge(squared, 1)
            chain.link(dve.tensor_scalar(stat[:, 1, :], stat[:, 0, :], 1.0 / D, EPS, ALU.mult, ALU.add))
            dve.reciprocal(stat[:, 2, :], stat[:, 1, :]).then_inc(inverted, 1)
            dve.wait_ge(rooted, 1)
            for h in range(2):
                cols = slice(h * half, (h + 1) * half)
                dve.tensor_scalar(xn[:, 0, cols], c.x[:, 0, cols], stat[:, 3, 0:1], None, ALU.mult).then_inc(scaled[0], 1)
            for b in range(8):
                dve.wait_ge(high, b + 1)
                for k in range(2):
                    kt = 2 * b + k
                    dve.scalar_tensor_tensor(out=c.hl[:, kt, :], in0=c.bank[b][:, k * S:(k + 1) * S],
                                             scalar=c.gain[:, gain_col + kt:gain_col + kt + 1],
                                             in1=c.hh[:, kt, :].bitcast(F32), op0=ALU.mult, op1=ALU.subtract)

        @block.tensor
        def _(pe):
            for b in range(8):
                if b % 4 == 0:
                    for t in range(TB):
                        pe.wait_ge(scaled[t], b // 4 + 1)
                for k in range(2):
                    for t in range(TB):
                        kt = 2 * b + k
                        ins = pe.transpose(c.bank[b][:, k * S + t * P:k * S + (t + 1) * P],
                                           xn[:, t, kt * P:(kt + 1) * P], c.ident[:, :])
                ins.then_inc(turned, 1)



def transpose_job(c, pe, job, bank):
    at = 0
    for piece in job[0]:
        n, wd = piece.shape[0], piece.shape[1]
        ins = pe.transpose(bank[0:wd, at:at + n], piece, c.ident[0:n, 0:n])
        at += n
    return ins


def take_job(act, job, bank):
    pieces, dst, factor = job
    src = bank[0:pieces[0].shape[1], 0:sum(p.shape[0] for p in pieces)]
    if factor is None:
        return act.activation(dst, src, ACT.Silu)
    return act.activation(dst, src, ACT.Copy, scale=factor)


class Side:

    def __init__(self, wait=0, lag=2):
        self.wait, self.lag = wait, lag
        self.before, self.scalar, self.vector, self.jobs = None, {}, {}, {}


def token_product(c, lhs, n_groups, per_group, take, row=None, ahead=(), make_side=None):
    st, sb, sem = stage(c)
    u0 = c.u0
    n = n_groups * per_group
    with st:
        taken = sem("taken")
        row_loaded = sem("row_loaded") if row else None
        side = make_side(sb, sem, taken) if make_side else Side()
        own, turned, cleared = (sem(x) for x in ("own", "turned", "cleared")) if make_side else (None,) * 3
        jobs = [(g, job) for g in range(n_groups) for job in side.jobs.get(g, ())]
        first_late = n_groups - (1 if side.lag < per_group else 2)
        assert all(len(side.jobs.get(g, ())) <= 4 for g in range(first_late))
        left = {}
        block = st.enter_context(c.nc.Block())

        def group_before(j):
            g, rest = divmod(j - side.lag, per_group)
            return g - 1 if rest == 0 else -1

        def take_group(dve, g):
            dve.wait_ge(c.w_used, u0 + (g + 1) * per_group)
            if row and g == 0:
                dve.wait_ge(row_loaded, 16)
            for t in range(TB):
                take(dve, g, c.bank[2 * (g % 2) + t], t).then_inc(taken, 1)

        @block.sync
        def _(sp):
            if row:
                broadcast_row(sp, row[0], row[1], row_loaded)
            for j in range(n):
                load_unit(c, sp, u0 + j + RAW)
                if j == n // 4:
                    preload(c, sp, ahead)

        @block.scalar
        def _(act):
            def side_work(g):
                if g in side.scalar:
                    side.scalar[g](act)

            def take_jobs(group):
                for i, (g, job) in enumerate(jobs):
                    if g == group:
                        act.wait_ge(turned, i + 1)
                        take_job(act, job, c.bank[4 + i % 4]).then_inc(cleared, 1)

            split_high(c, act, u0 + 1)
            for j in range(n):
                if j < n - 1:
                    split_high(c, act, u0 + j + AHEAD)
                if j % per_group == 0:
                    side_work(j // per_group - 1)
                take_jobs(group_before(j))
            side_work(n_groups - 1)
            for g in range(first_late, n_groups):
                take_jobs(g)

        @block.vector
        def _(dve):
            chain = Chain(dve, own)
            if side.before:
                side.before(chain)

            def side_work(g, i):
                if g in side.vector and 0 <= i < len(side.vector[g]):
                    if i == 0:
                        dve.wait_ge(taken, 2 * (g + 1))
                    side.vector[g][i](chain)
                left[g] = chain.n

            split_low(c, dve, u0 + 1)
            for j in range(n):
                if j < n - 1:
                    split_low(c, dve, u0 + j + AHEAD)
                side_work(j // per_group - 1, j % per_group - side.wait)
                if j % per_group == per_group - 1:
                    take_group(dve, j // per_group)
            for i in range(len(side.vector.get(n_groups - 1, ()))):
                side_work(n_groups - 1, i)
            left[n_groups - 1] = chain.n

        @block.tensor
        def _(pe):
            def transposes(group):
                for i, (g, job) in enumerate(jobs):
                    if g == group:
                        pe.wait_ge(taken, 2 * (g + 1))
                        if left[g]:
                            pe.wait_ge(own, left[g])
                        if i >= 4:
                            pe.wait_ge(cleared, i - 3)
                        transpose_job(c, pe, job, c.bank[4 + i % 4]).then_inc(turned, 1)

            for g in range(n_groups):
                if g >= 2:
                    pe.wait_ge(taken, 2 * (g - 1))
                for q in range(per_group):
                    u = u0 + g * per_group + q
                    transposes(group_before(g * per_group + q))
                    pe.wait_ge(c.w_low, u + 1)
                    wh, wl = split_view(c, u)
                    cols = wh.shape[2]
                    for t in range(TB):
                        out = c.bank[2 * (g % 2) + t][:, 0:cols]
                        for k in range(4):
                            ah, al = lhs(4 * q + k)
                            ins = three(pe, out, ah[:, t * P:(t + 1) * P], al[:, t * P:(t + 1) * P],
                                        wh[:, k, :], wl[:, k, :], q == 0 and k == 0, q == per_group - 1 and k == 3)
                    ins.then_inc(c.w_used, 1)
            for g in range(first_late, n_groups):
                transposes(g)
    c.u0 += n


def add_to_x(c):
    def take(dve, g, bank, t):
        cols = c.x[:, t, g * 512:(g + 1) * 512]
        return dve.tensor_tensor(cols, bank[:, :], cols, ALU.add)
    return take


def h_chunk(c):
    return lambda k: (c.hh[:, k, :], c.hl[:, k, :])


def y_chunk(c):
    return lambda k: (c.yh[:, k, :], c.yl[:, k, :])



def ffn(c, layer):
    norm_stage(c, GAIN_FFN + layer * KT)
    st, sb, sem = stage(c)
    with st:
        cv = sb("cv", [P, 2, 4, S])
        sg = sb("sg", [P, 2, 2, S])
        centred, conv, silu, gated, rounded, lowered, own, taken = (sem(x) for x in (
            "centred", "conv", "silu", "gated", "rounded", "lowered", "own", "taken"))
        block = st.enter_context(c.nc.Block())

        parts = []
        u = c.u0
        for part in FFN_PARTS:
            parts.append((u, (0 if not parts else parts[-1][1] + parts[-1][2]), part // 2, 4 * len(parts)))
            u += 2 * part + part
        end = u
        taps = c.conv[layer]


        def columns(n, half, k, s0):
            return c.w["w_up"][layer][k * P:(k + 8) * P, bass.ds((n + s0) * 256 + half * FF, 256)]\
                .rearrange("(k p) n -> p k n", p=P)

        @block.sync
        def _(sp):
            for u0, s0, slabs, _ in parts:
                for j in range(4):
                    load_unit(c, sp, u0 + j + RAW)
                with sp.Fori(0, slabs // 2 - 1) as i:
                    for j in range(4, 12):
                        load_unit(c, sp, u0 + j + RAW, i, 8, columns(i * 2 + (j // 4 + 1), (j % 4) // 2, (j % 2) * 8, s0))
                for j in range(4 * (slabs - 1), 6 * slabs):
                    load_unit(c, sp, u0 + j + RAW)

        @block.scalar
        def _(act):
            def centre(n0, s0, i=0):
                par = n0 % 2
                for q in range(4):
                    ch = (q // 2) * FFC + 2 * (s0 + n0) + q % 2
                    act.activation(cv[:, par, q, :], c.bank[2 * par + q // 2][:, (q % 2) * S:(q % 2 + 1) * S],
                                   ACT.Identity, bias=taps[:, 3, bass.ds(i * 2 + ch, 1)],
                                   scale=taps[:, 1, bass.ds(i * 2 + ch, 1)]).then_inc(centred, 1)

            def after(j, u0, s0, n0, i=0):
                if j == 1:
                    act.wait_ge(c.w_used, u0 + 4 * (n0 + 1) + i * 4)
                    centre(n0, s0, i)
                elif j == 2:
                    act.wait_ge(conv, s0 + n0 + 3 + i)
                    g = cv[:, n0 % 2, 0:2, :]
                    act.activation(g, g, ACT.Silu).then_inc(silu, 1)
                elif j == 3:
                    act.wait_ge(gated, s0 + n0 + 1 + i)
                    act.activation(c.yh[:, bass.ds(i * 2 + 2 * n0, 2), :], sg[:, n0 % 2, :, :], ACT.Copy).then_inc(rounded, 1)

            split_high(c, act, parts[0][0] + 1)
            for u0, s0, slabs, g0 in parts:
                for j in range(4):
                    split_high(c, act, u0 + j + AHEAD)
                with act.Fori(0, slabs - 2, 2) as i:
                    for s in (1, 2):
                        for j in range(4):
                            split_high(c, act, u0 + 4 * s + j + AHEAD, i, 4)
                            after(j, u0, s0, s - 1, i)
                for j in range(4):
                    split_high(c, act, u0 + 4 * (slabs - 1) + j + AHEAD)
                    after(j, u0, s0, slabs - 2)
                for j in range(2 * slabs):
                    after(j + 1, u0, s0, slabs - 1)
                    if u0 + 4 * slabs + j + AHEAD <= end:
                        split_high(c, act, u0 + 4 * slabs + j + AHEAD)

        @block.vector
        def _(dve):
            def after(j, u0, s0, n0, i=0):
                par = n0 % 2
                if j == 1:
                    dve.wait_ge(centred, 4 * (s0 + n0 + 1) + i * 4)
                    for tap, src, dst in ((0, slice(0, S - 1), slice(1, S)), (2, slice(1, S), slice(0, S - 1))):
                        for q in range(4):
                            ch = (q // 2) * FFC + 2 * (s0 + n0) + q % 2
                            v = c.bank[2 * par + q // 2][:, (q % 2) * S:(q % 2 + 1) * S]
                            out = cv[:, par, q, dst]
                            if tap:
                                dve.wait_ge(own, 4 * (s0 + n0) + q + 1 + i * 4)
                            ins = dve.scalar_tensor_tensor(out=out, in0=v[:, src], scalar=taps[:, tap, bass.ds(i * 2 + ch, 1)],
                                                           in1=out, op0=ALU.mult, op1=ALU.add)
                            if not tap:
                                ins.then_inc(own, 1)
                    ins.then_inc(conv, 1)
                elif j == 2:
                    dve.wait_ge(silu, s0 + n0 + 1 + i)
                    dve.tensor_tensor(sg[:, par, :, :], cv[:, par, 0:2, :], cv[:, par, 2:4, :], ALU.mult).then_inc(gated, 1)
                elif j == 3:
                    dve.wait_ge(rounded, s0 + n0 + 1 + i)
                    at = bass.ds(i * 2 + 2 * n0, 2)
                    dve.tensor_tensor(c.yl[:, at, :], sg[:, par, :, :], c.yh[:, at, :].bitcast(F32),
                                      ALU.subtract).then_inc(lowered, 1)

            def take(u0, slabs, g):
                per = slabs // 2
                dve.wait_ge(c.w_used, u0 + 4 * slabs + (g + 1) * per)
                for t in range(TB):
                    cols = c.x[:, t, g * 512:(g + 1) * 512]
                    dve.tensor_tensor(cols, c.bank[4 + 2 * (g % 2) + t][:, :], cols, ALU.add).then_inc(taken, 1)

            last = None
            dve.sem_inc(conv, 2)
            split_low(c, dve, parts[0][0] + 1)
            for u0, s0, slabs, g0 in parts:
                for j in range(4):
                    split_low(c, dve, u0 + j + AHEAD)
                    if j == 1 and last:
                        take(*last, 3)
                with dve.Fori(0, slabs - 2, 2) as i:
                    for s in (1, 2):
                        for j in range(4):
                            split_low(c, dve, u0 + 4 * s + j + AHEAD, i, 4)
                            after(j, u0, s0, s - 1, i)
                for j in range(4):
                    split_low(c, dve, u0 + 4 * (slabs - 1) + j + AHEAD)
                    after(j, u0, s0, slabs - 2)
                per = slabs // 2
                for j in range(2 * slabs):
                    after(j + 1, u0, s0, slabs - 1)
                    if u0 + 4 * slabs + j + AHEAD <= end:
                        split_low(c, dve, u0 + 4 * slabs + j + AHEAD)
                    if j >= per and j % per == 1:
                        take(u0, slabs, j // per - 1)
                last = (u0, slabs)
            take(*last, 3)

        @block.tensor
        def _(pe):
            def slab(u0, s0, n0, i=0):
                par = n0 % 2
                pe.wait_ge(conv, s0 + n0 + 1 + i)
                for q in range(4):
                    u = u0 + 4 * n0 + q
                    pe.wait_ge(c.w_low, u + 1 + i * 4)
                    wh, wl = split_view(c, u)
                    for m in range(2):
                        out = c.bank[2 * par + q // 2][:, m * S:(m + 1) * S]
                        for k in range(8):
                            kt = (q % 2) * 8 + k
                            ins = three(pe, out, wh[:, k, m * P:(m + 1) * P], wl[:, k, m * P:(m + 1) * P],
                                        c.hh[:, kt, :], c.hl[:, kt, :],
                                        kt == 0 and m == 0, kt == 15 and m == 1, skip=True)
                    ins.then_inc(c.w_used, 1)

            def down(u0, s0, slabs, g0):
                per = slabs // 2
                for g in range(4):
                    if g0 + g >= 2:
                        pe.wait_ge(taken, 2 * (g0 + g - 1))
                    for q in range(per):
                        u = u0 + 4 * slabs + g * per + q
                        pe.wait_ge(c.w_low, u + 1)
                        if g == 0:
                            pe.wait_ge(lowered, s0 + 2 * (q + 1))
                        wh, wl = split_view(c, u)
                        for t in range(TB):
                            out = c.bank[4 + 2 * (g % 2) + t][:, :]
                            for k in range(4):
                                ins = three(pe, out, c.yh[:, 4 * q + k, t * P:(t + 1) * P],
                                            c.yl[:, 4 * q + k, t * P:(t + 1) * P], wh[:, k, :], wl[:, k, :],
                                            q == 0 and k == 0, q == per - 1 and k == 3)
                        ins.then_inc(c.w_used, 1)

            for u0, s0, slabs, g0 in parts:
                slab(u0, s0, 0)
                with pe.Fori(0, slabs - 2, 2) as i:
                    for s in (1, 2):
                        slab(u0, s0, s, i)
                slab(u0, s0, slabs - 1)
                down(u0, s0, slabs, g0)

    c.u0 = u



def turn_stage(c, jobs):
    st, sb, sem = stage(c)
    with st:
        turned, taken = sem("turned"), sem("taken")
        block = st.enter_context(c.nc.Block())

        @block.tensor
        def _(pe):
            for j, job in enumerate(jobs):
                if j >= 8:
                    pe.wait_ge(taken, j - 7)
                transpose_job(c, pe, job, c.bank[j % 8]).then_inc(turned, 1)

        @block.scalar
        def _(act):
            for j, job in enumerate(jobs):
                act.wait_ge(turned, j + 1)
                take_job(act, job, c.bank[j % 8]).then_inc(taken, 1)


def head_pieces(p, t_cols, heads):
    return [p[:, t, t_cols + h * P:t_cols + (h + 1) * P] for h in heads for t in range(TB)]



def attention(c, units, joint=False):
    st, sb, sem = stage(c)
    ns = len(units[0]["segs"])
    nu = len(units)
    nout = ns if joint else 1
    ahead = 1 if ns == 1 else 0
    with st:
        prob = sb("prob", [P, 2, ns, TB, S])
        prob_t = sb("prob_t", [P, 2, ns, TB, S])
        top = sb("top", [P, 2, ns, TB])
        neg = sb("neg", [P, 2, ns, TB])
        tot = sb("tot", [P, 2, ns, TB])
        rec = sb("rec", [P, 2, ns, TB])
        out = sb("out", [P, nout, S])
        scored, masked, exped, weighted, turned, copied, valued, gated, rounded, lowered, joined, own = (sem(x) for x in (
            "scored", "masked", "exped", "weighted", "turned", "copied", "valued", "gated", "rounded", "lowered", "joined", "own"))
        block = st.enter_context(c.nc.Block())

        def s_bank(g):
            return c.bank[g % 3]

        def t_bank(g):
            return c.bank[3 + g % 2]

        def o_bank(n, s):
            return c.bank[5 + s] if joint else c.bank[5 + n % 2]

        @block.tensor
        def _(pe):
            def scores(n):
                for s, seg in enumerate(units[n]["segs"]):
                    g = n * ns + s
                    if g >= 3:
                        pe.wait_ge(masked, g - 2)
                    for qb in range(TB):
                        pairs = seg["score"](qb)
                        for i, (a, b) in enumerate(pairs):
                            ins = pe.matmul(s_bank(g)[:, qb * S:qb * S + seg["keys"]], a, b,
                                            start=i == 0, stop=i == len(pairs) - 1)
                    ins.then_inc(scored, 1)

            def turns(n):
                for s, seg in enumerate(units[n]["segs"]):
                    g = n * ns + s
                    pe.wait_ge(weighted, g + 1)
                    if g >= 2:
                        pe.wait_ge(copied, g - 1)
                    keys = seg["keys"]
                    for kb in range(max(1, keys // P)):
                        k = min(keys, P)
                        for qb in range(TB):
                            ins = pe.transpose(t_bank(g)[0:k, kb * S + qb * P:kb * S + (qb + 1) * P],
                                               prob[:, n % 2, s, qb, kb * P:kb * P + k], c.ident[:, :])
                    ins.then_inc(turned, 1)

            def values(n):
                for s, seg in enumerate(units[n]["segs"]):
                    pe.wait_ge(copied, n * ns + s + 1)
                    if s == 0 and n >= (1 if joint else 2):
                        pe.wait_ge(gated, (n if joint else n - 1) * nout)
                    k, blocks = min(seg["keys"], P), max(1, seg["keys"] // P)
                    for kb in range(blocks):
                        ins = pe.matmul(o_bank(n, s)[:, 0:S], seg["value"](kb), prob_t[0:k, n % 2, s, kb, :],
                                        start=kb == 0 and (joint or s == 0),
                                        stop=kb == blocks - 1 and (joint or s == ns - 1))
                    if joint or s == ns - 1:
                        ins.then_inc(valued, 1)

            if ahead:
                scores(0)
            for n in range(nu + 2):
                if n + ahead < nu:
                    scores(n + ahead)
                if n >= 2:
                    values(n - 2)
                if 1 <= n <= nu:
                    turns(n - 1)

        @block.vector
        def _(dve):
            chain = Chain(dve, own)

            def maxima(n):
                b = n % 2
                if n >= 2:
                    dve.wait_ge(turned, (n - 1) * ns)
                for s, seg in enumerate(units[n]["segs"]):
                    g = n * ns + s
                    dve.wait_ge(scored, g + 1)
                    for qb in range(TB):
                        src = s_bank(g)[:, qb * S:qb * S + seg["keys"]]
                        dst = prob[:, b, s, qb, 0:seg["keys"]]
                        if seg["mask"] is None:
                            ins = dve.tensor_scalar(dst, src, 1.0, None, ALU.mult, ALU.max, accum_out=top[:, b, s, qb:qb + 1])
                        else:
                            ins = dve.tensor_tensor_reduce(dst, src, seg["mask"][:, qb, :], 1.0, -3e38, ALU.add,
                                                           ALU.max, top[:, b, s, qb:qb + 1])
                    chain.link(ins)
                    dve.tensor_scalar(neg[:, b, s, :], top[:, b, s, :], -1.0, None, ALU.mult).then_inc(masked, 1)
                if joint:
                    dve.wait_ge(masked, (n + 1) * ns)
                    chain.link(dve.tensor_tensor(neg[:, b, 0, :], neg[:, b, 0, :], neg[:, b, 1, :], ALU.min))
                    dve.tensor_tensor(neg[:, b, 0, :], neg[:, b, 0, :], neg[:, b, 2, :], ALU.min).then_inc(joined, 1)

            def weights(n):
                b = n % 2
                dve.wait_ge(exped, (n + 1) * ns)
                if joint:
                    chain.link(dve.tensor_tensor(tot[:, b, 0, :], tot[:, b, 0, :], tot[:, b, 1, :], ALU.add))
                    chain.link(dve.tensor_tensor(tot[:, b, 0, :], tot[:, b, 0, :], tot[:, b, 2, :], ALU.add))
                    chain.link(dve.reciprocal(rec[:, b, 0, :], tot[:, b, 0, :]))
                else:
                    chain.link(dve.reciprocal(rec[:, b, :, :], tot[:, b, :, :]))
                for s, seg in enumerate(units[n]["segs"]):
                    r = 0 if joint else s
                    if seg["weight"] is not None:
                        chain.link(dve.tensor_tensor(rec[:, b, s, :], rec[:, b, s, :], seg["weight"], ALU.mult))
                    for qb in range(TB):
                        pr = prob[:, b, s, qb, 0:seg["keys"]]
                        if seg["keep"] is None:
                            ins = dve.tensor_scalar(pr, pr, rec[:, b, r, qb:qb + 1], None, ALU.mult)
                        else:
                            ins = dve.scalar_tensor_tensor(out=pr, in0=pr, scalar=rec[:, b, r, qb:qb + 1],
                                                           in1=seg["keep"][:, qb, :], op0=ALU.mult, op1=ALU.mult)
                    ins.then_inc(weighted, 1)

            def output(n):
                for s in range(nout):
                    m = n * nout + s
                    dve.wait_ge(valued, m + 1)
                    if m >= nout:
                        dve.wait_ge(lowered, m - nout + 1)
                    src = o_bank(n, s)[:, 0:S]
                    if units[n]["gate"] is None:
                        dve.tensor_copy(out[:, s, :], src).then_inc(gated, 1)
                    else:
                        dve.tensor_tensor(out[:, s, :], src, units[n]["gate"], ALU.mult).then_inc(gated, 1)

            def low(n):
                for s in range(nout):
                    dve.wait_ge(rounded, n * nout + s + 1)
                    kt = units[n]["out"][s]
                    dve.tensor_tensor(c.yl[:, kt, :], out[:, s, :], c.yh[:, kt, :].bitcast(F32),
                                      ALU.subtract).then_inc(lowered, 1)

            for n in range(nu + 3):
                if n < nu:
                    maxima(n)
                if 1 <= n <= nu:
                    weights(n - 1)
                if 3 <= n:
                    low(n - 3)
                if 2 <= n <= nu + 1:
                    output(n - 2)

        @block.scalar
        def _(act):
            def exps(n):
                b = n % 2
                for s, seg in enumerate(units[n]["segs"]):
                    if joint and s == 0:
                        act.wait_ge(joined, n + 1)
                    elif not joint:
                        act.wait_ge(masked, n * ns + s + 1)
                    r = 0 if joint else s
                    for qb in range(TB):
                        pr = prob[:, b, s, qb, 0:seg["keys"]]
                        ins = act.activation(pr, pr, ACT.Exp, bias=neg[:, b, r, qb:qb + 1],
                                             accum_out=tot[:, b, s, qb:qb + 1])
                    ins.then_inc(exped, 1)

            def copies(n):
                for s, seg in enumerate(units[n]["segs"]):
                    g = n * ns + s
                    if g >= 2 * ns:
                        act.wait_ge(valued, (n - 1) * nout)
                    act.wait_ge(turned, g + 1)
                    k, w = min(seg["keys"], P), max(1, seg["keys"] // P) * S
                    act.activation(prob_t[0:k, n % 2, s, :, :].rearrange("p a q -> p (a q)")[:, 0:w],
                                   t_bank(g)[0:k, 0:w], ACT.Copy).then_inc(copied, 1)

            def high(n):
                for s in range(nout):
                    act.wait_ge(gated, n * nout + s + 1)
                    act.activation(c.yh[:, units[n]["out"][s], :], out[:, s, :], ACT.Copy).then_inc(rounded, 1)

            for n in range(nu + 2):
                if n < nu:
                    exps(n)
                if 1 <= n <= nu:
                    copies(n - 1)
                if n >= 2:
                    high(n - 2)



def mixer_a(c, consts):
    nh = A_HEADS + A_KV
    with ExitStack() as outer:
        rb = scoped(c, outer, "a")
        qkv = rb("qkv", [P, TB, nh * P + A_KV * P])
        tab = rb("rope_tab", [P, 2, TB, P])
        gains = rb("rope_gain", [P, 2, P])
        norm_stage(c, GAIN_MIX, ahead=[(tab[:, :, :, :], consts["a_rope"])] + [
            (gains[:, i, :], c.w[name][0:1, :].broadcast_to([P, P])) for i, name in enumerate(("a_q_gain", "a_k_gain"))])
        qk_t = rb("qk_t", [P, nh, S])

        def take(dve, g, bank, t):
            return dve.tensor_copy(qkv[:, t, g * 512:(g + 1) * 512], bank[:, :])

        def pair(ap, i):
            return ap.rearrange("p (a b f) -> p a b f", a=2, b=2)[:, :, i, :]

        def make_side(sb, sem, taken):
            side = Side(wait=1, lag=5)
            tg = sb("tab_gain", [P, 2, 2, TB, P])
            part = sb("part", [P, 4, P])
            square = sb("square", [P, P])
            stat = sb("stat", [P, 2, TB, 6, 4])
            summed, rooted = sem("summed"), sem("rooted")

            def tables(chain):
                dve = chain.eng
                await_preloads(c, dve)
                for i in range(2):
                    for t in range(TB):
                        dve.tensor_tensor(tg[:, 0, i, t, :], tab[:, 0, t, :], gains[:, i, :], ALU.mult)
                        for b in range(2):
                            ins = dve.tensor_tensor(pair(tg[:, 1, i, t, :], b), pair(tab[:, 1, t, :], b),
                                                    pair(gains[:, i, :], 1 - b), ALU.mult)
                chain.link(ins)

            def rms(g):
                def work(act):
                    act.wait_ge(taken, 2 * (g + 1))
                    for t in range(TB):
                        for h in range(4):
                            a0 = (4 * g + h) * P
                            act.activation(square[:, :], qkv[:, t, a0:a0 + P], ACT.Square,
                                           accum_out=stat[:, 0, t, g, h:h + 1]).then_inc(summed, 1)
                            act.wait_ge(summed, 8 * g + 4 * t + h + 1)
                    act.activation(stat[:, 1, :, g, :], stat[:, 0, :, g, :], ACT.Sqrt, scale=1.0 / P,
                                   bias=c.eps[:, 0:1]).then_inc(rooted, 1)
                return work

            def rotation(g):
                i = g // 4
                x3 = [qkv[:, t, g * 512:(g + 1) * 512].rearrange("p (h d) -> p h d", d=P) for t in range(TB)]

                def normalise(chain, t):
                    chain.link(chain.eng.tensor_tensor(x3[t], x3[t], stat[:, 0, t, g, :].unsqueeze(2)
                                                       .broadcast_to([P, 4, P]), ALU.mult))

                def partners(chain, t):
                    for b in range(2):
                        ins = chain.eng.tensor_tensor(
                            part[:, :, :].rearrange("p h (a b f) -> p h a b f", a=2, b=2)[:, :, :, b, :],
                            x3[t].rearrange("p h (a b f) -> p h a b f", a=2, b=2)[:, :, :, 1 - b, :],
                            pair(tg[:, 1, i, t, :], b).unsqueeze(1).broadcast_to([P, 4, 2, 32]), ALU.mult)
                    chain.link(ins)

                def cosine(chain, t):
                    chain.link(chain.eng.tensor_tensor(x3[t], x3[t], tg[:, 0, i, t, :].unsqueeze(1)
                                                       .broadcast_to([P, 4, P]), ALU.mult))

                def add(chain, t):
                    chain.link(chain.eng.tensor_tensor(x3[t], x3[t], part[:, :, :], ALU.add))

                def first(chain):
                    chain.eng.wait_ge(rooted, g + 1)
                    chain.link(chain.eng.reciprocal(stat[:, 0, :, g, :], stat[:, 1, :, g, :]))
                    normalise(chain, 0)
                    partners(chain, 0)

                def second(chain):
                    cosine(chain, 0)
                    add(chain, 0)
                    normalise(chain, 1)

                def third(chain):
                    partners(chain, 1)
                    cosine(chain, 1)
                    add(chain, 1)

                return [first, second, third]

            side.before = tables
            for g in range(nh // 4):
                side.scalar[g], side.vector[g] = rms(g), rotation(g)
                side.jobs[g] = [(head_pieces(qkv, 0, (h, h + 1)), both(qk_t[:, h:h + 2, :]),
                                 P ** -0.5 if h < A_HEADS else 1.0) for h in (4 * g, 4 * g + 2)]
            return side

        token_product(c, h_chunk(c), 6, 4, take, make_side=make_side)

        def unit(h):
            kv = A_HEADS + h // (A_HEADS // A_KV)
            return dict(segs=[dict(
                keys=S, mask=None, keep=None, weight=None,
                score=lambda qb: [(qk_t[:, h, qb * P:(qb + 1) * P], qk_t[:, kv, :])],
                value=lambda kb: qkv[:, kb, (kv + A_KV) * P:(kv + A_KV + 1) * P])], gate=None, out=[h])

        attention(c, [unit(h) for h in range(A_HEADS)])
    token_product(c, y_chunk(c), 4, 4, add_to_x(c))



def bias_stage(c, consts, scratch):
    st, sb, sem = stage(c)
    with st:
        table = sb("bucket_bias", [33, B_GROUPS * B_HEADS])
        hot = sb("bucket_hot", [33, B_GROUPS, 2 * S])
        rows = sb("bias_rows", [B_HEADS, B_GROUPS, 2 * S])
        loaded, filled, product, copied, stored = (sem(x) for x in ("loaded", "filled", "product", "copied", "stored"))
        block = st.enter_context(c.nc.Block())

        @block.sync
        def _(sp):
            sp.dma_start(table[0:32, :], c.w["rel_bias"]).then_inc(loaded, 16)
            sp.dma_start(hot[:, :, :], consts["b_hot"]).then_inc(loaded, 16)
            sp.wait_ge(copied, 3)
            sp.dma_start(scratch[0].rearrange("(g h) n -> h g n", g=B_GROUPS), rows[:, :, :]).then_inc(stored, 16)
            sp.wait_ge(stored, 16)
            skewed = bass.AP(scratch[1].tensor, 0, [[SKEW, B_GROUPS * B_HEADS], [2 * S + 1, P], [1, 2 * S]])
            sp.dma_start(skewed, scratch[0].unsqueeze(1).broadcast_to([B_GROUPS * B_HEADS, P, 2 * S])).then_inc(c.skewed, 16)

        @block.vector
        def _(dve):
            dve.memset(table[32:33, :], 1.0).then_inc(filled, 1)
            for g in range(B_GROUPS):
                dve.wait_ge(product, g + 1)
                dve.tensor_copy(rows[:, g, :], c.bank[g][0:B_HEADS, :]).then_inc(copied, 1)

        @block.tensor
        def _(pe):
            pe.wait_ge(loaded, 32)
            pe.wait_ge(filled, 1)
            for g in range(B_GROUPS):
                pe.matmul(c.bank[g][0:B_HEADS, :], table[:, g * B_HEADS:(g + 1) * B_HEADS], hot[:, g, :],
                          start=True, stop=True).then_inc(product, 1)


def b_project(c, scratch, q_t, k_t, v, bias, first_head):
    st, sb, sem = stage(c)
    u0 = c.u0
    slabs = 3 * B_GROUPS
    with st:
        taken, biased = sem("taken"), sem("biased")
        block = st.enter_context(c.nc.Block())

        @block.sync
        def _(sp):
            sp.wait_ge(c.skewed, 16)
            for i in range(2):
                for g in range(B_GROUPS):
                    row = g * B_HEADS + first_head + i
                    for t in range(TB):
                        src = bass.AP(scratch[1].tensor, row * SKEW + S - 1 - t * P, [[2 * S, P], [1, S]])
                        sp.dma_start(bias[:, i, g, t, :], src).then_inc(biased, 16)
            load_steps(c, sp, 2 * slabs)
            sp.wait_ge(biased, 16 * 2 * B_GROUPS * TB)

        @block.scalar
        def _(act):
            def take(m):
                act.wait_ge(c.w_used, u0 + 2 * (m + 1))
                g, kind = m // 3, m % 3
                bank = c.bank[m % 4][:, :]
                if kind < 2:
                    dst = (q_t, k_t)[kind][:, g, :, :].rearrange("p h q -> p (h q)")
                    act.activation(dst, bank, ACT.Copy, scale=P ** -0.5 if kind == 0 else 1.0).then_inc(taken, 1)
                else:
                    act.activation(v[:, :, g, :], bank.rearrange("p (t n) -> p t n", t=TB), ACT.Copy).then_inc(taken, 1)

            split_high(c, act, u0 + 1)
            for m in range(slabs):
                split_high(c, act, u0 + 2 * m + AHEAD)
                if m < slabs - 1:
                    split_high(c, act, u0 + 2 * m + 1 + AHEAD)
                take(m)

        @block.vector
        def _(dve):
            for j in range(-1, 2 * slabs - 1):
                split_low(c, dve, u0 + j + AHEAD)

        @block.tensor
        def _(pe):
            for m in range(slabs):
                if m >= 4:
                    pe.wait_ge(taken, m - 3)
                for q in range(2):
                    u = u0 + 2 * m + q
                    pe.wait_ge(c.w_low, u + 1)
                    wh, wl = split_view(c, u)
                    for i in range(2):
                        out = c.bank[m % 4][:, i * S:(i + 1) * S]
                        for k in range(8):
                            kt = 8 * q + k
                            if m % 3 < 2:
                                ops = (wh[:, k, i * P:(i + 1) * P], wl[:, k, i * P:(i + 1) * P], c.hh[:, kt, :], c.hl[:, kt, :])
                            else:
                                ops = (c.hh[:, kt, i * P:(i + 1) * P], c.hl[:, kt, i * P:(i + 1) * P], wh[:, k, :], wl[:, k, :])
                            ins = three(pe, out, *ops, kt == 0 and i == 0, kt == 15 and i == 1, skip=True)
                    ins.then_inc(c.w_used, 1)
    c.u0 += 2 * slabs


def mixer_b(c, consts, scratch):
    norm_stage(c, GAIN_MIX + KT)
    outer = ExitStack()
    with outer:
        def sb(name, shape):
            return outer.enter_context(c.nc.sbuf_tensor(name, shape, F32))

        q_t = sb("b_q_t", [P, B_GROUPS, 2, S])
        k_t = sb("b_k_t", [P, B_GROUPS, 2, S])
        v = sb("b_v", [P, TB, B_GROUPS, 2 * P])
        bias = sb("b_bias", [P, 2, B_GROUPS, TB, S])
        for half in range(2):
            for pair in range(2):
                b_project(c, scratch, q_t, k_t, v, bias, half * 4 + pair * 2)

                def seg(i, g):
                    return dict(keys=S, mask=bias[:, i, g, :, :], keep=None, weight=None,
                                score=lambda qb: [(q_t[:, g, i, qb * P:(qb + 1) * P], k_t[:, g, i, :])],
                                value=lambda kb: v[:, kb, g, i * P:(i + 1) * P])

                attention(c, [dict(segs=[seg(i, g) for g in range(B_GROUPS)], gate=None,
                                   out=[g * 4 + pair * 2 + i for g in range(B_GROUPS)]) for i in range(2)], joint=True)
            token_product(c, y_chunk(c), 4, 3, add_to_x(c))



def broadcast_row(sp, dst, row, sem):
    sp.dma_start(dst, row.unsqueeze(0).broadcast_to([P, row.shape[0]])).then_inc(sem, 16)


def final_norm_stage(c):
    st, sb, sem = stage(c)
    with st:
        g = sb("final_gain", [P, D])
        sq = sb("final_sq", [P, TB, D])
        stat = sb("final_stat", [P, 4, TB])
        loaded, squared, inverted, rooted, own = (sem(x) for x in ("loaded", "squared", "inverted", "rooted", "own"))
        block = st.enter_context(c.nc.Block())

        @block.sync
        def _(sp):
            broadcast_row(sp, g[:, :], c.w["final_norm"], loaded)

        @block.scalar
        def _(act):
            for t in range(TB):
                act.activation(sq[:, t, :], c.x[:, t, :], ACT.Square, accum_out=stat[:, 0, t:t + 1]).then_inc(squared, 1)
            act.wait_ge(inverted, 1)
            act.activation(stat[:, 3, :], stat[:, 2, :], ACT.Sqrt).then_inc(rooted, 1)

        @block.vector
        def _(dve):
            chain = Chain(dve, own)
            dve.wait_ge(squared, 2)
            chain.link(dve.tensor_scalar(stat[:, 1, :], stat[:, 0, :], 1.0 / D, EPS, ALU.mult, ALU.add))
            dve.reciprocal(stat[:, 2, :], stat[:, 1, :]).then_inc(inverted, 1)
            dve.wait_ge(rooted, 1)
            dve.wait_ge(loaded, 16)
            for t in range(TB):
                dve.scalar_tensor_tensor(out=c.x[:, t, :], in0=c.x[:, t, :], scalar=stat[:, 3, t:t + 1], in1=g[:, :],
                                         op0=ALU.mult, op1=ALU.mult)



def project_part(c, layer, index, p, brow, jobs=(), ahead=(), work=None, lag=2):
    name, width, groups = PARTS[index]
    first = sum(q[1] for q in PARTS[:index])
    starts = [sum(groups[:g]) for g in range(len(groups))]

    def take(dve, g, bank, t):
        a, b = starts[g], starts[g] + groups[g]
        return dve.tensor_tensor(p[:, t, a:b], bank[:, 0:groups[g]], brow[:, a:b], ALU.add)

    def group_of(end):
        return next(g for g in range(len(groups)) if end <= starts[g] + groups[g])

    def make_side(sb, sem, taken):
        side = Side(lag=lag)
        for end, scalar, vector in (work(sb, sem, taken) if work else ()):
            assert group_of(end) not in side.vector
            side.vector[group_of(end)] = vector
            if scalar:
                side.scalar[group_of(end)] = scalar
        for end, job in jobs:
            side.jobs.setdefault(group_of(end), []).append(job)
        return side

    token_product(c, h_chunk(c), len(groups), 4, take, row=(brow[:, :], c.w["b_in_2"][layer, first:first + width]),
                  ahead=ahead, make_side=make_side)


def both(ap):
    return ap.rearrange("p h q -> p (h q)")


def head_jobs(p, col, heads, dst, factor):
    return [(col + (h + 2) * P, (head_pieces(p, col, (h, h + 1)), both(dst[:, h:h + 2, :]), factor))
            for h in range(0, heads, 2)]


def rotate(chain, x3, tab, t, heads, width, part):
    dve, hw = chain.eng, width // 2
    for b in range(2):
        o, q = b * hw, (1 - b) * hw
        chain.link(dve.tensor_tensor(part[:, 0:heads, o:o + hw], x3[:, :, q:q + hw],
                                     tab[:, 1, t, o:o + hw].unsqueeze(1).broadcast_to([P, heads, hw]), ALU.mult))
    chain.link(dve.tensor_tensor(x3, x3, tab[:, 0, t, 0:width].unsqueeze(1).broadcast_to([P, heads, width]), ALU.mult))
    chain.link(dve.tensor_tensor(x3, x3, part[:, 0:heads, 0:width], ALU.add))


def stick_breaking(c, q_t, k_t, value, gate_t, strict, out0):
    st, sb, sem = stage(c)
    with st:
        a = sb("sb_a", [P, H2, TB, S])
        r = sb("sb_r", [P, H2, TB, S])
        w_t = sb("sb_w_t", [P, 2, TB, S])
        out = sb("sb_out", [P, 2, S])
        (scored, sized, exped, logged, summed, powered, weighted, turned, copied, valued, gated, rounded, own) = (
            sem(x) for x in ("scored", "sized", "exped", "logged", "summed", "powered", "weighted", "turned",
                             "copied", "valued", "gated", "rounded", "own"))
        block = st.enter_context(c.nc.Block())

        @block.tensor
        def _(pe):
            for h in range(H2):
                for qb in range(TB):
                    ins = pe.matmul(c.bank[h][:, qb * S:(qb + 1) * S], q_t[:, h, qb * P:(qb + 1) * P], k_t[:, h, :],
                                    start=True, stop=True)
                ins.then_inc(scored, 1)

            def turns(h):
                pe.wait_ge(weighted, h + 1)
                if h >= 2:
                    pe.wait_ge(copied, h - 1)
                for kb in range(TB):
                    for qb in range(TB):
                        ins = pe.transpose(c.bank[4 + h % 2][:, kb * S + qb * P:kb * S + (qb + 1) * P],
                                           r[:, h, qb, kb * P:(kb + 1) * P], c.ident[:, :])
                ins.then_inc(turned, 1)

            def values(h):
                pe.wait_ge(copied, h + 1)
                if h >= 2:
                    pe.wait_ge(gated, h - 1)
                for kb in range(TB):
                    ins = pe.matmul(c.bank[6 + h % 2][:, 0:S], value(h, kb), w_t[:, h % 2, kb, :], start=kb == 0, stop=kb == 1)
                ins.then_inc(valued, 1)

            for n in range(H2 + 1):
                if n >= 1:
                    values(n - 1)
                if n < H2:
                    turns(n)

        @block.scalar
        def _(act):
            for h in range(H2):
                act.wait_ge(scored, h + 1)
                act.activation(both(a[:, h, :, :]), c.bank[h][:, :], ACT.Abs).then_inc(sized, 1)
            for h in range(H2):
                act.wait_ge(sized, h + 1)
                act.activation(a[:, h, :, :], a[:, h, :, :], ACT.Exp, scale=-1.0).then_inc(exped, 1)
            for h in range(H2):
                act.wait_ge(exped, h + 1)
                act.activation(a[:, h, :, :], a[:, h, :, :], ACT.Ln, bias=1.0).then_inc(logged, 1)

            def power(h):
                act.wait_ge(summed, h + 1)
                act.activation(r[:, h, :, :], r[:, h, :, :], ACT.Exp).then_inc(powered, 1)

            def copy(h):
                act.wait_ge(turned, h + 1)
                act.activation(both(w_t[:, h % 2, :, :]), c.bank[4 + h % 2][:, :], ACT.Copy).then_inc(copied, 1)

            def high(h):
                act.wait_ge(gated, h + 1)
                act.activation(c.yh[:, out0 + h, :], out[:, h % 2, :], ACT.Copy).then_inc(rounded, 1)

            for n in range(H2 + 2):
                if n < H2:
                    power(n)
                if 1 <= n <= H2:
                    copy(n - 1)
                if n >= 2:
                    high(n - 2)

        @block.vector
        def _(dve):
            chain = Chain(dve, own)
            await_preloads(c, dve)

            def sums(h):
                dve.wait_ge(logged, h + 1)
                chain.link(dve.scalar_tensor_tensor(out=both(a[:, h, :, :]), in0=c.bank[h][:, :], scalar=0.0,
                                                    in1=both(a[:, h, :, :]), op0=ALU.max, op1=ALU.add))
                chain.link(dve.tensor_tensor(a[:, h, :, :], a[:, h, :, :], strict[:, 0, :, :], ALU.mult))
                for qb in range(TB):
                    ins = dve.tensor_tensor_scan(r[:, h, qb, ::-1], strict[:, 1, qb, ::-1], a[:, h, qb, ::-1], 0.0,
                                                 ALU.mult, ALU.add)
                chain.link(ins)
                dve.tensor_tensor(both(r[:, h, :, :]), c.bank[h][:, :], both(r[:, h, :, :]), ALU.subtract).then_inc(summed, 1)

            def weights(h):
                dve.wait_ge(powered, h + 1)
                dve.tensor_tensor(r[:, h, :, :], r[:, h, :, :], strict[:, 0, :, :], ALU.mult).then_inc(weighted, 1)

            def gate(h):
                dve.wait_ge(valued, h + 1)
                dve.tensor_tensor(out[:, h % 2, :], c.bank[6 + h % 2][:, 0:S], gate_t[:, h, :], ALU.mult).then_inc(gated, 1)

            def low(h):
                dve.wait_ge(rounded, h + 1)
                dve.tensor_tensor(c.yl[:, out0 + h, :], out[:, h % 2, :], c.yh[:, out0 + h, :].bitcast(F32), ALU.subtract)

            for n in range(H2 + 3):
                if n < H2:
                    sums(n)
                if 1 <= n <= H2:
                    weights(n - 1)
                if n >= 3:
                    low(n - 3)
                if 2 <= n <= H2 + 1:
                    gate(n - 2)


def scoped(c, outer, tag):
    def sb(name, shape, dt=F32):
        return outer.enter_context(c.nc.sbuf_tensor(f"{tag}_{name}", shape, dt))
    return sb


def mixer_sb(c, layer, consts):
    with ExitStack() as outer:
        sb = scoped(c, outer, f"sb{layer}")
        p = sb("p", [P, TB, 2048])
        q_t, k_t, gate_t = sb("q_t", [P, H2, S]), sb("k_t", [P, H2, S]), sb("gate_t", [P, H2, S])
        strict = sb("strict", [P, 2, TB, S])
        with ExitStack() as inner:
            project_part(c, layer, 0, p, scoped(c, inner, f"sb{layer}")("brow", [P, 2048]),
                         head_jobs(p, 0, H2, q_t, P ** -0.5) + head_jobs(p, 512, H2, k_t, 1.0)
                         + head_jobs(p, 1536, H2, gate_t, None), ahead=[(strict[:, :, :, :], consts["strict"])])
        stick_breaking(c, q_t, k_t, lambda h, kb: p[:, kb, 1024 + h * P:1024 + (h + 1) * P], gate_t, strict, 0)


def compress_stage(c, tok_t, small, comp, cmp_tab, w1k, w1v, w1v_rows, w2):
    st, sb, sem = stage(c)
    with st:
        nb = 32 * N_CMP
        blk = [c.conv_all[:, 0:nb].rearrange("p (j n) -> p j n", n=N_CMP), sb("cmp_blk", [P, 32, N_CMP])]
        hid = c.conv_all[:, nb:nb + 2 * N_CMP].rearrange("p (i n) -> p i n", i=2)
        part = c.conv_all[:, nb + 2 * N_CMP:nb + 2 * N_CMP + P].unsqueeze(1)
        made, product, activated, first_half, rest, own = (sem(x) for x in (
            "made", "product", "activated", "first_half", "rest", "own"))
        block = st.enter_context(c.nc.Block())

        @block.sync
        def _(sp):
            sp.dma_start(w1v[:, :, :], w1v_rows[:, 0:16, :]).then_inc(first_half, 16)
            sp.wait_ge(product, 1)
            sp.dma_start(w1k[:, 0:16, :], w1v_rows[:, 16:32, :]).then_inc(rest, 16)

        @block.vector
        def _(dve):
            chain = Chain(dve, own)
            for i in range(2):
                base = tok_t[:, i, :]
                src = bass.AP(base.tensor, base.offset, [list(base.ap[0]), [1, 32], [16, N_CMP]])
                dve.tensor_tensor(blk[i][:, :, :], src, small[:, i * 32:(i + 1) * 32].unsqueeze(2)
                                  .broadcast_to([P, 32, N_CMP]), ALU.add).then_inc(made, 1)
            for i in range(2):
                dve.wait_ge(product, 3 + i)
                chain.link(dve.tensor_copy(comp[:, i, :], c.bank[2 + i][0:N_CMP, 0:P]))
            k = comp[:, 0:1, :]
            for b in range(2):
                o, q = b * 64, (1 - b) * 64
                chain.link(dve.tensor_tensor(part[0:N_CMP, :, o:o + 64], k[:, :, q:q + 64],
                                             cmp_tab[:, 1:2, o:o + 64], ALU.mult))
            chain.link(dve.tensor_tensor(k, k, cmp_tab[:, 0:1, :], ALU.mult))
            chain.link(dve.tensor_tensor(k, k, part[0:N_CMP, :, :], ALU.add))

        @block.tensor
        def _(pe):
            pe.wait_ge(made, 2)
            await_preloads(c, pe)
            for i in range(2):
                for j in range(32):
                    if i == 1 and j % 16 == 0:
                        pe.wait_ge((first_half, rest)[j // 16], 16)
                    w1 = w1v[:, j, :] if i == 1 and j < 16 else w1k[:, j % 16 if i else j, :]
                    ins = pe.matmul(c.bank[i][:, 0:N_CMP], w1, blk[i][:, j, :], start=j == 0, stop=j == 31)
                ins.then_inc(product, 1)
            for i in range(2):
                pe.wait_ge(activated, i + 1)
                pe.matmul(c.bank[2 + i][0:N_CMP, 0:P], hid[:, i, :], w2[:, i, :], start=True, stop=True).then_inc(product, 1)

        @block.scalar
        def _(act):
            for i in range(2):
                act.wait_ge(product, i + 1)
                act.activation(hid[:, i, :], c.bank[i][:, 0:N_CMP], ACT.Silu).then_inc(activated, 1)


def rotate_stage(c, x3, tab, heads, width):
    st, sb, sem = stage(c)
    with st:
        part = sb("rot_part", [P, heads, width])
        own = sem("own")
        block = st.enter_context(c.nc.Block())

        @block.vector
        def _(dve):
            chain = Chain(dve, own)
            for t in range(TB):
                rotate(chain, x3(t), tab, t, heads, width, part)


def mixer_nsa(c, layer, consts, small):
    with ExitStack() as outer:
        sb = scoped(c, outer, f"nsa{layer}")
        p = sb("p", [P, TB, 1804])
        q_t, gate_t, ks_t = sb("q_t", [P, H2, S]), sb("gate_t", [P, H2, S]), sb("ks_t", [P, 2, S])
        tok_t = sb("tok_t", [P, 2, S])
        branch = sb("branch", [P, TB, 3 * H2])
        comp, kc_t = sb("comp", [N_CMP, 2, P]), sb("kc_t", [P, N_CMP])
        cmask = sb("cmask", [P, 2, TB, N_CMP])
        cmp_tab = sb("cmp_tab", [N_CMP, 2, P])
        weights = ExitStack()
        w1k = scoped(c, weights, f"nsa{layer}")("w1k", [P, 32, P])
        w2 = scoped(c, weights, f"nsa{layer}")("w2", [P, 2, P])
        tab = scoped(c, weights, f"nsa{layer}")("tab", [P, 2, TB, P])

        def w1_rows(name):
            return c.w[name][layer].rearrange("(j d) m -> d j m", d=P)

        def heads(col, n):
            return lambda t: p[:, t, col:col + n * P].rearrange("p (h d) -> p h d", d=P)

        def work(sb, sem, taken):
            part = sb("rot_part", [P, 4, P])

            def rotation(col, n, t):
                def vector(chain):
                    if col == 0 and t == 0:
                        await_preloads(c, chain.eng)
                    rotate(chain, heads(col, n)(t), tab, t, n, P, part)
                return vector

            def keys(col):
                def vector(chain):
                    for t in range(TB):
                        rotation(col, 1, t)(chain)
                return vector

            def sigmoid(act):
                act.wait_ge(taken, 2 * 3)
                act.activation(branch[:, :, :], p[:, :, 1280:1292], ACT.Sigmoid)

            return [(896, None, [rotation(0, H2, 0), keys(768), rotation(0, H2, 1)]), (1292, sigmoid, [keys(1024)])]

        with ExitStack() as inner:
            project_part(c, layer, 1, p, scoped(c, inner, f"nsa{layer}")("brow", [P, 1804]),
                         [(896, job) for _, job in head_jobs(p, 0, H2, q_t, P ** -0.5)] + head_jobs(p, 512, 2, tok_t, 1.0)
                         + [(col + P, (head_pieces(p, col, (0,)), ks_t[:, i, :], 1.0)) for i, col in enumerate((768, 1024))]
                         + head_jobs(p, 1292, H2, gate_t, None), work=work, lag=4,
                         ahead=[(tab[:, :, :, :], consts["rope"]), (cmask[:, :, :, :], consts["cmask"]),
                                (cmp_tab[:, :, :], consts["cmp_rope"]), (w1k[:, :, :], w1_rows("nsa_cmp_w1_k_2")),
                                (w2[:, 0, :], c.w["nsa_cmp_w2_k_2"][layer]), (w2[:, 1, :], c.w["nsa_cmp_w2_v_2"][layer])])
        w1v = scoped(c, weights, f"nsa{layer}")("w1v", [P, 16, P])

        compress_stage(c, tok_t, small, comp, cmp_tab, w1k, w1v, w1_rows("nsa_cmp_w1_v_2"), w2)
        weights.close()
        turn_stage(c, [([comp[:, 0, :]], kc_t[:, :], 1.0)])

        def seg(h, b):
            base = dict(weight=branch[:, :, h * 3 + b], keep=None, mask=c.causal, keys=S)
            if b == 0:
                return base | dict(keys=N_CMP, mask=cmask[:, 0, :, :], keep=cmask[:, 1, :, :],
                                   score=lambda qb: [(q_t[:, h, qb * P:(qb + 1) * P], kc_t[:, :])],
                                   value=lambda kb: comp[:, 1, :])
            v0 = 896 if b == 1 else 1152
            return base | dict(score=lambda qb: [(q_t[:, h, qb * P:(qb + 1) * P], ks_t[:, b - 1, :])],
                               value=lambda kb: p[:, kb, v0:v0 + P])

        attention(c, [dict(segs=[seg(h, b) for b in range(3)], gate=gate_t[:, h, :], out=[4 + h]) for h in range(H2)])


def forget_work(c, p, fb, forget):
    def work(sb, sem, taken):
        f = sb("fox_f", [P, 3, TB, H2])
        sized, exped, logged = sem("sized"), sem("exped"), sem("logged")

        def vector(chain):
            dve = chain.eng
            await_preloads(c, dve)
            for t in range(TB):
                chain.link(dve.tensor_tensor(f[:, 0, t, :], p[:, t, 1536:1540], fb[:, :], ALU.add))
            dve.scalar_tensor_tensor(out=f[:, 1, :, :], in0=f[:, 0, :, :], scalar=-1.0, in1=f[:, 0, :, :],
                                     op0=ALU.mult, op1=ALU.min).then_inc(sized, 1)
            dve.wait_ge(logged, 1)
            chain.link(dve.tensor_scalar(f[:, 0, :, :], f[:, 0, :, :], -1.0, 0.0, ALU.mult, ALU.max))
            chain.link(dve.tensor_tensor(f[:, 2, :, :], f[:, 0, :, :], f[:, 1, :, :], ALU.add))
            for t in range(TB):
                ins = dve.tensor_copy(forget[:, t, :, :], f[:, 2, t, :].unsqueeze(2).broadcast_to([P, H2, P]))
            chain.link(ins)

        def scalar(act):
            act.wait_ge(sized, 1)
            act.activation(f[:, 1, :, :], f[:, 1, :, :], ACT.Exp).then_inc(exped, 1)
            act.wait_ge(exped, 1)
            act.activation(f[:, 1, :, :], f[:, 1, :, :], ACT.Ln, bias=1.0).then_inc(logged, 1)

        return [(1540, scalar, [vector])]
    return work


def mixer_fox(c, layer, consts):
    with ExitStack() as outer:
        sb = scoped(c, outer, f"fox{layer}")
        p = sb("p", [P, TB, 2052])
        q_t, k_t, gate_t = sb("q_t", [P, H2, S]), sb("k_t", [P, H2, S]), sb("gate_t", [P, H2, S])
        upper = sb("upper", [P, TB, S])
        fb = sb("fb", [P, H2])
        forget = sb("forget", [P, TB, H2, P])
        with ExitStack() as inner:
            project_part(c, layer, 2, p, scoped(c, inner, f"fox{layer}")("brow", [P, 2052]),
                         head_jobs(p, 0, H2, q_t, P ** -0.5) + head_jobs(p, 512, H2, k_t, 1.0)
                         + head_jobs(p, 1540, H2, gate_t, None), work=forget_work(c, p, fb, forget),
                         ahead=[(upper[:, :, :], consts["upper"]),
                                (fb[:, :], c.w["fox_forget_bias_2"][layer].unsqueeze(0).broadcast_to([P, H2]))])

        def unit(h):
            return dict(segs=[dict(
                keys=S, mask=c.causal, keep=None, weight=None,
                score=lambda qb: [(q_t[:, h, qb * P:(qb + 1) * P], k_t[:, h, :])]
                + [(forget[:, t, h, :], upper[:, t, :]) for t in range(TB)],
                value=lambda kb: p[:, kb, 1024 + h * P:1024 + (h + 1) * P])], gate=gate_t[:, h, :], out=[8 + h])

        attention(c, [unit(h) for h in range(H2)])


def latent_work(c, p, tab):
    spans = ((0, 384), (384, 512))

    def work(sb, sem, taken):
        sq = sb("lat_sq", [P, 384])
        part = sb("rot_part", [P, 1, 64])
        stat = sb("lat_stat", [P, 3, TB, 2])
        inverted, rooted = sem("inverted"), sem("rooted")

        def squares(chain):
            dve = chain.eng
            for t in range(TB):
                for i, (a, b) in enumerate(spans):
                    x = p[:, t, a:b]
                    chain.link(dve.tensor_tensor_reduce(sq[:, 0:b - a], x, x, 1.0, 0.0, ALU.mult, ALU.add, stat[:, 0, t, i:i + 1]))
            for i, (a, b) in enumerate(spans):
                chain.link(dve.tensor_scalar(stat[:, 1, :, i], stat[:, 0, :, i], 1.0 / (b - a), EPS, ALU.mult, ALU.add))
            dve.reciprocal(stat[:, 2, :, :], stat[:, 1, :, :]).then_inc(inverted, 1)

        def rotary(chain):
            await_preloads(c, chain.eng)
            for t in range(TB):
                rotate(chain, p[:, t, 512:576].unsqueeze(1), tab, t, 1, 64, part)

        def scaling(chain):
            dve = chain.eng
            dve.wait_ge(rooted, 1)
            for t in range(TB):
                for i, (a, b) in enumerate(spans):
                    ins = dve.tensor_scalar(p[:, t, a:b], p[:, t, a:b], stat[:, 0, t, i:i + 1], None, ALU.mult)
            chain.link(ins)

        def scalar(act):
            act.wait_ge(inverted, 1)
            act.activation(stat[:, 0, :, :], stat[:, 2, :, :], ACT.Sqrt).then_inc(rooted, 1)

        return [(576, scalar, [squares, rotary, scaling])]
    return work


def expand_stage(c, lat_t, q, kv, w_uq, w_ukv):
    st, sb, sem = stage(c)
    with st:
        product = sem("product")
        block = st.enter_context(c.nc.Block())

        @block.tensor
        def _(pe):
            await_preloads(c, pe)
            for t in range(TB):
                for half in range(2):
                    for k in range(3):
                        ins = pe.matmul(c.bank[4 * t + half][:, 0:384], lat_t[:, k, t * P:(t + 1) * P],
                                        w_uq[:, k, half * 384:(half + 1) * 384], start=k == 0, stop=k == 2)
                    ins.then_inc(product, 1)
                for half in range(2):
                    pe.matmul(c.bank[4 * t + 2 + half][:, :], lat_t[:, 3, t * P:(t + 1) * P],
                              w_ukv[:, half * 512:(half + 1) * 512], start=True, stop=True).then_inc(product, 1)

        @block.vector
        def _(dve):
            for t in range(TB):
                for half in range(2):
                    dve.wait_ge(product, 4 * t + half + 1)
                    dve.tensor_copy(q[:, t, half * 384:(half + 1) * 384], c.bank[4 * t + half][:, 0:384])
                for half in range(2):
                    dve.wait_ge(product, 4 * t + 2 + half + 1)
                    dve.tensor_copy(kv[:, t, half * 512:(half + 1) * 512], c.bank[4 * t + 2 + half][:, :])


def mixer_mla(c, layer, consts, small):
    with ExitStack() as outer:
        sb = scoped(c, outer, f"mla{layer}")
        p = sb("p", [P, TB, 1088])
        gate_t, lat_t = sb("gate_t", [P, H2, S]), sb("lat_t", [P, 4, S])
        kr_t = sb("kr_t", [64, S])
        q, kv = sb("q", [P, TB, 768]), sb("kv", [P, TB, 1024])
        tab = sb("tab", [P, 2, TB, 64])
        weights = ExitStack()
        w_uq = scoped(c, weights, f"mla{layer}")("w_uq", [P, 3, 768])
        w_ukv = scoped(c, weights, f"mla{layer}")("w_ukv", [P, 1024])
        with ExitStack() as inner:
            project_part(c, layer, 3, p, scoped(c, inner, f"mla{layer}")("brow", [P, 1088]),
                         [(576, (head_pieces(p, k * P, (0,)), lat_t[:, k, :], small[:, 64 + k:65 + k])) for k in range(4)]
                         + [(832, ([p[:, t, 512:576] for t in range(TB)], kr_t[:, :], 1.0))]
                         + head_jobs(p, 576, H2, gate_t, None), work=latent_work(c, p, tab), lag=4,
                         ahead=[(tab[:, :, :, :], consts["rope64"]),
                                (w_uq[:, :, :], c.w["mla_w_uq_2"][layer].rearrange("(k p) n -> p k n", p=P)),
                                (w_ukv[:, :], c.w["mla_w_ukv_2"][layer])])
        expand_stage(c, lat_t, q, kv, w_uq, w_ukv)
        weights.close()
        q_t, k_t = sb("q_t", [P, H2, S]), sb("k_t", [P, H2, S])
        qr_t = sb("qr_t", [64, H2, S])
        rotate_stage(c, lambda t: q[:, t, :].rearrange("p (h d) -> p h d", d=192)[:, :, P:192], tab, H2, 64)
        scale = 192 ** -0.5
        turn_stage(c, [([q[:, t, h * 192:h * 192 + P] for t in range(TB)], q_t[:, h, :], scale) for h in range(H2)]
                   + [([q[:, t, h * 192 + P:(h + 1) * 192] for t in range(TB)], qr_t[:, h, :], scale) for h in range(H2)]
                   + [([kv[:, t, h * 256:h * 256 + P] for t in range(TB)], k_t[:, h, :], 1.0) for h in range(H2)])

        def unit(h):
            return dict(segs=[dict(
                keys=S, mask=c.causal, keep=None, weight=None,
                score=lambda qb: [(q_t[:, h, qb * P:(qb + 1) * P], k_t[:, h, :]),
                                  (qr_t[:, h, qb * P:(qb + 1) * P], kr_t[:, :])],
                value=lambda kb: kv[:, kb, h * 256 + P:(h + 1) * 256])], gate=gate_t[:, h, :], out=[12 + h])

        attention(c, [unit(h) for h in range(H2)])


def post_stage(c, layer, o):
    st, sb, sem = stage(c)
    with st:
        g = sb("post_gain", [P, D])
        sq = sb("post_sq", [P, D])
        stat = sb("post_stat", [P, 4, TB])
        loaded, squared, inverted, rooted, own = (sem(x) for x in ("loaded", "squared", "inverted", "rooted", "own"))
        block = st.enter_context(c.nc.Block())

        @block.sync
        def _(sp):
            broadcast_row(sp, g[:, :], c.w["post_norm_g_2"][layer], loaded)

        @block.scalar
        def _(act):
            for t in range(TB):
                if t:
                    act.wait_ge(squared, t)
                act.activation(sq[:, :], o[:, t, :], ACT.Square, accum_out=stat[:, 0, t:t + 1]).then_inc(squared, 1)
            act.wait_ge(inverted, 1)
            act.activation(stat[:, 3, :], stat[:, 2, :], ACT.Sqrt).then_inc(rooted, 1)

        @block.vector
        def _(dve):
            chain = Chain(dve, own)
            dve.wait_ge(squared, 2)
            chain.link(dve.tensor_scalar(stat[:, 1, :], stat[:, 0, :], 1.0 / D, EPS, ALU.mult, ALU.add))
            dve.reciprocal(stat[:, 2, :], stat[:, 1, :]).then_inc(inverted, 1)
            dve.wait_ge(rooted, 1)
            dve.wait_ge(loaded, 16)
            for t in range(TB):
                chain.link(dve.scalar_tensor_tensor(out=o[:, t, :], in0=o[:, t, :], scalar=stat[:, 3, t:t + 1],
                                                    in1=g[:, :], op0=ALU.mult, op1=ALU.mult))
                dve.tensor_tensor(c.x[:, t, :], c.x[:, t, :], o[:, t, :], ALU.add)


def hybrid_layer(c, layer, consts):
    norm_stage(c, GAIN_PRE + layer * KT)
    mixer_sb(c, layer, consts)
    mixer_nsa(c, layer, consts, c.small[layer])
    mixer_fox(c, layer, consts)
    mixer_mla(c, layer, consts, c.small[layer])
    with ExitStack() as outer:
        o = scoped(c, outer, f"hy{layer}")("o", [P, TB, D])
        token_product(c, y_chunk(c), 4, 4,
                      lambda dve, g, bank, t: dve.tensor_copy(o[:, t, g * 512:(g + 1) * 512], bank[:, :]))
        post_stage(c, layer, o)


def store_stage(c, out):
    st, sb, sem = stage(c)
    with st:
        stored = sem("stored")
        block = st.enter_context(c.nc.Block())

        @block.sync
        def _(sp):
            sp.dma_start(out[0].rearrange("(t p) d -> p t d", p=P), c.x[:, :, :]).then_inc(stored, 16)
            sp.wait_ge(stored, 16)


def build(nc, w, consts, scratch, out, upto=99):
    with ExitStack() as ctx:
        c = make_core(nc, w, ctx)
        steps = [lambda: (setup_stage(c, consts), bias_stage(c, consts, scratch)), lambda: mixer_a(c, consts), lambda: ffn(c, 0),
                 lambda: mixer_b(c, consts, scratch), lambda: ffn(c, 1), lambda: final_norm_stage(c),
                 lambda: hybrid_layer(c, 0, consts), lambda: hybrid_layer(c, 1, consts)]
        for step in steps[:upto]:
            step()
        store_stage(c, out)
        c.sems.close()


def constants():
    f = np.float32
    q = np.arange(S)[:, None]
    k = np.arange(S)[None, :]

    def tiled(m):
        return np.ascontiguousarray(m.reshape(TB, P, -1).transpose(1, 0, 2)).astype(f)

    def tables(pos, half):
        inv = (f(10000.0) ** (-np.arange(half, dtype=f) / f(half))).astype(f)
        ang = pos.astype(f)[:, None] * inv[None, :]
        co, si = np.cos(ang), np.sin(ang)
        return np.concatenate([co, co], 1), np.concatenate([-si, si], 1)

    def both_tables(a, b):
        return np.ascontiguousarray(np.stack([tiled(a), tiled(b)], 1)).astype(f)

    t = np.arange(S)
    rows, cols = tables(t // 64, 32), tables(t % 64, 32)
    cmp_end = np.arange(N_CMP) * 16 + 31
    seen = cmp_end[None, :] <= q
    hot = np.zeros((33, B_GROUPS, 2 * S), f)
    for g, (window, dil) in enumerate(((128, 1), (512, 4), (2048, 16))):
        for j in range(2 * S - 1):
            rel = j - (S - 1)
            if rel % dil or abs(rel) // dil > window // (2 * dil):
                hot[32, g, j] = NEG
                continue
            n = abs(rel)
            large = 8 + int(np.log(f(max(n, 1)) / f(8)) / f(np.log(1024 / 8)) * f(8))
            hot[(16 if rel > 0 else 0) + (n if n < 8 else min(large, 15)), g, j] = 1.0
    return {
        "ident": np.eye(P, dtype=f),
        "causal": tiled(np.where(k <= q, 0.0, NEG)),
        "strict": np.ascontiguousarray(np.stack([tiled(k < q), tiled(k < q - 1)], 1)),
        "upper": tiled(q <= k),
        "a_rope": both_tables(np.concatenate([rows[0], cols[0]], 1), np.concatenate([rows[1], cols[1]], 1)),
        "rope": both_tables(*tables(t, 64)),
        "rope64": both_tables(*tables(t, 32)),
        "cmp_rope": np.ascontiguousarray(np.stack(tables(cmp_end, 64), 1)).astype(f),
        "cmask": np.ascontiguousarray(np.stack([tiled(np.where(seen, 0.0, NEG)), tiled(seen)], 1)).astype(f),
        "b_hot": hot,
    }


def kernel(**inputs):
    from concourse import bacc
    from concourse.bass_utils import run_bass_kernel_spmd

    nc = bacc.Bacc("TRN2", target_bir_lowering=False, num_devices=1)
    arrays, w, consts = {}, {}, {}
    for name, a in inputs.items():
        arrays[f"in_{name}"] = np.ascontiguousarray(a)
        w[name] = nc.dram_tensor(f"in_{name}", a.shape, F32, kind="ExternalInput").ap()
    for name, a in constants().items():
        arrays[f"const_{name}"] = a
        consts[name] = nc.dram_tensor(f"const_{name}", a.shape, F32, kind="ExternalInput").ap()
    scratch = [nc.dram_tensor(name, shape, F32, kind="Internal").ap() for name, shape in (
        ("bias_rows", (B_GROUPS * B_HEADS, 2 * S)), ("bias_skewed_rows", (B_GROUPS * B_HEADS, SKEW)))]
    out = nc.dram_tensor("out", (1, S, D), F32, kind="ExternalOutput").ap()
    build(nc, w, consts, scratch, out)
    r = run_bass_kernel_spmd(nc, [arrays], core_ids=[0])
    return r.results[0]["out"]
```
